# Optimizing a Trainium2 kernel written in Bass

```python
import math
import jax, jax.numpy as jnp
from jax import lax
import numpy as np

D_MODEL = 1024
BATCH = 1
SEQ = 1024
DEPTH = 2

CHUNK = 64
Q_BLOCK = 128
EPS = 1e-6
A_HEADS = D_MODEL // 128
A_HEAD_DIM = 64
A_V_DIM = 2 * A_HEAD_DIM
B_HEAD_DIM = 64
B_Q_HEADS = D_MODEL // B_HEAD_DIM
B_KV_HEADS = 4
B_GROUP = B_Q_HEADS // B_KV_HEADS
WINDOW = 128
WINDOW_CHUNKS = WINDOW // CHUNK
D_FF = 4 * D_MODEL
N_A = (DEPTH + 1) // 2
N_B = DEPTH - N_A

kernel_name = "yoco_diffattn_swa_sink_alibi_trunk"

def rms_norm(x, g):
    xf = x.astype(jnp.float32)
    y = xf * lax.rsqrt(jnp.mean(xf * xf, axis=-1, keepdims=True) + EPS)
    return (y * g.astype(jnp.float32)).astype(x.dtype)

def alibi_slopes(n_heads):
    i = jnp.arange(1, n_heads + 1, dtype=jnp.float32)
    return jnp.exp2(-8.0 * i / n_heads)

def sq_relu_mlp(h, w_up, w_down):
    u = jax.nn.relu(h @ w_up)
    return (u * u) @ w_down

def diff_attention(h, w_qkv, q_g, k_g, lq1, lk1, lq2, lk2, subln_g, w_o, lambda_init):
    b, s, _ = h.shape
    qk_w = A_HEADS * 2 * A_HEAD_DIM
    qkv = h @ w_qkv
    q = qkv[..., :qk_w].reshape(b, s, A_HEADS, 2, A_HEAD_DIM)
    k = qkv[..., qk_w:2 * qk_w].reshape(b, s, A_HEADS, 2, A_HEAD_DIM)
    v = qkv[..., 2 * qk_w:].reshape(b, s, A_HEADS, A_V_DIM)
    q = rms_norm(q, q_g) * (A_HEAD_DIM ** -0.5)
    k = rms_norm(k, k_g)
    f32 = jnp.float32
    lam = (jnp.exp(jnp.sum(lq1.astype(f32) * lk1.astype(f32)))
           - jnp.exp(jnp.sum(lq2.astype(f32) * lk2.astype(f32))) + lambda_init)
    slopes = alibi_slopes(A_HEADS)
    pos = jnp.arange(s)
    nqb = s // Q_BLOCK
    qb = jnp.moveaxis(q.reshape(b, nqb, Q_BLOCK, A_HEADS, 2, A_HEAD_DIM), 1, 0)

    def attend_block(args):
        q_blk, blk = args
        qpos = blk * Q_BLOCK + jnp.arange(Q_BLOCK)
        logits = jnp.einsum('bqhcd,bkhcd->bhcqk', q_blk, k).astype(f32)
        dist = jnp.abs(qpos[:, None] - pos[None, :]).astype(f32)
        allowed = (pos[None, :] // CHUNK) <= (qpos[:, None] // CHUNK)
        logits = logits - slopes[None, :, None, None, None] * dist
        logits = jnp.where(allowed, logits, -jnp.inf)
        p = jax.nn.softmax(logits, axis=-1)
        wts = p[:, :, 0] - lam * p[:, :, 1]
        return jnp.einsum('bhqk,bkhe->bqhe', wts.astype(v.dtype), v)

    o = lax.map(attend_block, (qb, jnp.arange(nqb)))
    o = jnp.moveaxis(o, 0, 1).reshape(b, s, A_HEADS, A_V_DIM)
    o = rms_norm(o, subln_g) * (1.0 - lambda_init)
    return o.reshape(b, s, A_HEADS * A_V_DIM) @ w_o

def shared_kv(h_stream, kv_norm_g, w_kv, k_g):
    b, s, _ = h_stream.shape
    kv = rms_norm(h_stream, kv_norm_g) @ w_kv
    kvw = B_KV_HEADS * B_HEAD_DIM
    k = kv[..., :kvw].reshape(b, s, B_KV_HEADS, B_HEAD_DIM)
    v = kv[..., kvw:].reshape(b, s, B_KV_HEADS, B_HEAD_DIM)
    return rms_norm(k, k_g), v

def swa_sink_attention(h, w_q, q_g, sinks, w_o, k, v):
    b, s, _ = h.shape
    nc = s // CHUNK
    wc = WINDOW_CHUNKS
    f32 = jnp.float32
    q = (h @ w_q).reshape(b, s, B_KV_HEADS, B_GROUP, B_HEAD_DIM)
    q = rms_norm(q, q_g) * (B_HEAD_DIM ** -0.5)
    qc = q.reshape(b, nc, CHUNK, B_KV_HEADS, B_GROUP, B_HEAD_DIM)
    pad = ((0, 0), (wc - 1, 0), (0, 0), (0, 0), (0, 0))
    kpad = jnp.pad(k.reshape(b, nc, CHUNK, B_KV_HEADS, B_HEAD_DIM), pad)
    vpad = jnp.pad(v.reshape(b, nc, CHUNK, B_KV_HEADS, B_HEAD_DIM), pad)
    kb = jnp.concatenate([kpad[:, j:j + nc] for j in range(wc)], axis=2)
    vb = jnp.concatenate([vpad[:, j:j + nc] for j in range(wc)], axis=2)
    c = jnp.arange(nc)
    qpos = c[:, None] * CHUNK + jnp.arange(CHUNK)[None, :]
    kpos = (c[:, None] - wc + 1) * CHUNK + jnp.arange(wc * CHUNK)[None, :]
    valid = kpos >= 0
    dist = jnp.abs(qpos[:, :, None] - kpos[:, None, :]).astype(f32)
    slopes = alibi_slopes(B_Q_HEADS).reshape(B_KV_HEADS, B_GROUP)
    logits = jnp.einsum('bnqhgd,bnkhd->bnhgqk', qc, kb).astype(f32)
    logits = logits - slopes[None, None, :, :, None, None] * dist[None, :, None, None, :, :]
    logits = jnp.where(valid[None, :, None, None, None, :], logits, -jnp.inf)
    sink = jnp.broadcast_to(sinks.astype(f32).reshape(1, 1, B_KV_HEADS, B_GROUP, 1, 1),
                            logits.shape[:-1] + (1,))
    p = jax.nn.softmax(jnp.concatenate([logits, sink], axis=-1), axis=-1)[..., :-1]
    o = jnp.einsum('bnhgqk,bnkhd->bnqhgd', p.astype(vb.dtype), vb)
    return o.reshape(b, s, B_Q_HEADS * B_HEAD_DIM) @ w_o

def setup_inputs(seed: int = 0) -> dict:
    key = jax.random.key(seed)
    ks = jax.random.split(key, 24)
    f32 = jnp.float32
    res_scale = (2.0 * DEPTH) ** -0.5

    def nrm(k, shape, scale):
        return jax.random.normal(k, shape, f32) * scale

    def gain(k, shape):
        return 1.0 + 0.05 * jax.random.normal(k, shape, f32)

    a_qkv_out = 2 * A_HEADS * 2 * A_HEAD_DIM + A_HEADS * A_V_DIM
    return {
        "x": jax.random.normal(ks[0], (BATCH, SEQ, D_MODEL), f32),
        "attn_norm_g": gain(ks[1], (DEPTH, D_MODEL)),
        "mlp_norm_g": gain(ks[2], (DEPTH, D_MODEL)),
        "a_w_qkv": nrm(ks[3], (N_A, D_MODEL, a_qkv_out), D_MODEL ** -0.5),
        "a_q_norm_g": gain(ks[4], (N_A, A_HEAD_DIM)),
        "a_k_norm_g": gain(ks[5], (N_A, A_HEAD_DIM)),
        "a_lambda_q1": nrm(ks[6], (N_A, A_HEAD_DIM), 0.1),
        "a_lambda_k1": nrm(ks[7], (N_A, A_HEAD_DIM), 0.1),
        "a_lambda_q2": nrm(ks[8], (N_A, A_HEAD_DIM), 0.1),
        "a_lambda_k2": nrm(ks[9], (N_A, A_HEAD_DIM), 0.1),
        "a_subln_g": gain(ks[10], (N_A, A_V_DIM)),
        "a_w_o": nrm(ks[11], (N_A, A_HEADS * A_V_DIM, D_MODEL), (A_HEADS * A_V_DIM) ** -0.5 * res_scale),
        "kv_norm_g": gain(ks[12], (D_MODEL,)),
        "w_kv": nrm(ks[13], (D_MODEL, 2 * B_KV_HEADS * B_HEAD_DIM), D_MODEL ** -0.5),
        "kv_k_norm_g": gain(ks[14], (B_HEAD_DIM,)),
        "b_w_q": nrm(ks[15], (N_B, D_MODEL, B_Q_HEADS * B_HEAD_DIM), D_MODEL ** -0.5),
        "b_q_norm_g": gain(ks[16], (N_B, B_HEAD_DIM)),
        "b_sinks": nrm(ks[17], (N_B, B_Q_HEADS), 1.0),
        "b_w_o": nrm(ks[18], (N_B, B_Q_HEADS * B_HEAD_DIM, D_MODEL), (B_Q_HEADS * B_HEAD_DIM) ** -0.5 * res_scale),
        "mlp_w_up": nrm(ks[19], (DEPTH, D_MODEL, D_FF), D_MODEL ** -0.5),
        "mlp_w_down": nrm(ks[20], (DEPTH, D_FF, D_MODEL), D_FF ** -0.5 * res_scale),
    }

def reference(x, attn_norm_g, mlp_norm_g, a_w_qkv, a_q_norm_g, a_k_norm_g, a_lambda_q1,
              a_lambda_k1, a_lambda_q2, a_lambda_k2, a_subln_g, a_w_o, kv_norm_g, w_kv,
              kv_k_norm_g, b_w_q, b_q_norm_g, b_sinks, b_w_o, mlp_w_up, mlp_w_down):
    k_sh = None
    v_sh = None
    for l in range(DEPTH):
        h = rms_norm(x, attn_norm_g[l])
        if l < N_A:
            lambda_init = 0.8 - 0.6 * math.exp(-0.3 * l)
            x = x + diff_attention(h, a_w_qkv[l], a_q_norm_g[l], a_k_norm_g[l],
                                   a_lambda_q1[l], a_lambda_k1[l], a_lambda_q2[l], a_lambda_k2[l],
                                   a_subln_g[l], a_w_o[l], lambda_init)
        else:
            j = l - N_A
            x = x + swa_sink_attention(h, b_w_q[j], b_q_norm_g[j], b_sinks[j], b_w_o[j], k_sh, v_sh)
        x = x + sq_relu_mlp(rms_norm(x, mlp_norm_g[l]), mlp_w_up[l], mlp_w_down[l])
        if l == N_A - 1:
            k_sh, v_sh = shared_kv(x, kv_norm_g, w_kv, kv_k_norm_g)
    return x


_drawn_inputs = setup_inputs


def setup_inputs(seed=0):
    import zlib

    import numpy as np

    out = dict(_drawn_inputs(seed))
    spreads = {}
    factors = {'a_q_norm_g': 3.183,
     'a_k_norm_g': 2.784,
     'a_lambda_q1': 5.37,
     'a_lambda_k2': 8.0,
     'kv_norm_g': 7.11,
     'kv_k_norm_g': 8.0,
     'b_q_norm_g': 8.0,
     'b_sinks': 8.0}
    for name, (base, spread) in spreads.items():
        noise = np.random.default_rng([zlib.crc32(name.encode()), seed]).standard_normal(out[name].shape)
        drawn = base * np.exp(spread * noise) if base else spread * noise
        out[name] = __import__('jax').numpy.asarray(drawn.astype(out[name].dtype))
    for name, factor in factors.items():
        out[name] = (out[name] * factor).astype(out[name].dtype)
    return out
```

```python
from contextlib import ExitStack

import concourse.bass as bass
import numpy as np
from concourse import mybir

ALU = mybir.AluOpType
ACT = mybir.ActivationFunctionType
F32 = mybir.dt.float32
F32R = mybir.dt.float32r
I32 = mybir.dt.int32
AX_X = mybir.AxisListType.X

P = 128
D = 1024
S = 1024
KC = D // P
NB = S // P
HALF = 512
NH = 8
HD = 64
KVH = 4
GRP = 4
CH = 64
FF = 4096
EPS = 1e-6
LAM0 = 0.2
QUARTERS = 4
SEG = KC + QUARTERS * 2 * KC
MASK = -1e30
LOWEST = -3.0e38
CONSTS = 19


def lag_banks(s):
    return s // 4 + 1


def plan_a(first_use, attn, tail, qkv):
    uses = {}
    n = first_use
    for s in range(NB):
        if (s == 0 and tail) or (s > 0 and attn):
            for i in range(lag_banks((s - 1) % NB)):
                uses["lag", s, i] = n
                n += 1
        if s % 2 == 0 and (attn if s == 0 else qkv):
            uses["pair", s] = n
            n += 1
        if s == 1 and tail:
            for i in range(2):
                uses["o", i] = n
                n += 1
    return uses, n


def plan_b(first0, first1, steps, has_lag):
    uses = {}
    n = [first0, first1]
    for s in steps:
        if (s >= 2 or has_lag) and (len(steps) == NB or s < 2):
            for b in range(2):
                if b == 1 or s != 2:
                    uses["p", s, b] = n[b]
                    n[b] += 1
        if s == 0 and len(steps) == NB:
            for b in range(2):
                uses["k", b] = n[b]
                n[b] += 1
    return uses, n


def trunk(nc, io):
    ctx = ExitStack()
    with ctx:
        def sb(name, shape, dt=F32, scope=ctx):
            return scope.enter_context(nc.sbuf_tensor(name, shape, dt))

        def sem(name):
            return ctx.enter_context(nc.semaphore(name))

        ident = sb("ident", [P, P])
        ones = sb("ones", [P, P])
        gains = sb("gains", [P, 5, KC])
        heads64 = sb("heads64", [P, 8])
        gsub = sb("gsub", [P, 1])
        lam_in = sb("lam_in", [HD, 4])
        lam_pr = sb("lam_pr", [HD, 2])
        lam_e = sb("lam_e", [P, 2])
        neg_lam = sb("neg_lam", [P, 1])
        sink_col = sb("sink_col", [16, 1])
        sink_dg = sb("sink_dg", [16, 16])
        sinks = sb("sinks", [P, 16])
        slopes = sb("slopes", [P, NH + 16])
        msq = sb("msq", [P, NB])
        row_r = sb("row_r", [P, NB])
        chain_v = sb("chain_v", [P, 8])
        chain_s = sb("chain_s", [P, 8], I32)
        chain_t = sb("chain_t", [P, 8])
        chain_q = sb("chain_q", [P, 8])
        stat_m = sb("stat_m", [P, 8])
        xT = sb("xT", [P, KC, S])
        oT = None
        base = ExitStack()

        scope_d = ExitStack()
        a_hi = sb("a_hi", [P, KC, S], F32R, scope_d)
        a_lo = sb("a_lo", [P, KC, S], F32R, scope_d)
        scope_d2 = ExitStack()
        b_hi = sb("b_hi", [P, KC, S], F32R, scope_d2)
        b_lo = sb("b_lo", [P, KC, S], F32R, scope_d2)
        scope_w = ExitStack()
        w_raw = [sb(f"w_raw{i}", [P, KC, P], F32, scope_w) for i in range(2)]
        w_hi = [sb(f"w_hi{i}", [P, KC, P], F32R, scope_w) for i in range(2)]
        w_lo = [sb(f"w_lo{i}", [P, KC, P], F32R, scope_w) for i in range(2)]
        e1 = [sb(f"e1_{i}", [P, HALF], F32, scope_w) for i in range(2)]
        e2 = [sb(f"e2_{i}", [P, HALF], F32, scope_w) for i in range(2)]
        ss = sb("ss", [P, S], F32, scope_w)
        r2 = sb("r2", [P, S], F32, scope_w)
        scope_w.close()
        scope_wb = ExitStack()
        wb_raw = sb("wb_raw", [P, KC, 256], F32, scope_wb)
        wb_hi = sb("wb_hi", [P, KC, 256], F32R, scope_wb)
        wb_lo = sb("wb_lo", [P, KC, 256], F32R, scope_wb)
        dist_b = sb("dist_b", [P, 256], F32, scope_wb)
        bias_b = sb("bias_b", [P, GRP, 256], F32, scope_wb)
        osb = [sb(f"osb{i}", [P, GRP, HD], F32, scope_wb) for i in range(2)]
        qraw_b = [sb(f"qraw_b{i}", [P, 256], F32, scope_wb) for i in range(2)]
        sq_b = sb("sq_b", [P, 256], F32, scope_wb)
        rstd_k = sb("rstd_k", [P, NB, KVH], F32, scope_wb)
        rstd_q = [sb(f"rstd_q{i}", [P, GRP], F32, scope_wb) for i in range(2)]
        mx_b = sb("mx_b", [P, GRP], F32, scope_wb)
        nm_b = [sb(f"nm_b{i}", [P, GRP], F32, scope_wb) for i in range(2)]
        esin_b = [sb(f"esin_b{i}", [P, GRP], F32, scope_wb) for i in range(2)]
        es_b = [sb(f"es_b{i}", [P, GRP], F32, scope_wb) for i in range(2)]
        sm_b = [sb(f"sm_b{i}", [P, GRP], F32, scope_wb) for i in range(2)]
        den_b = sb("den_b", [P, GRP], F32, scope_wb)
        rc_b = sb("rc_b", [P, GRP], F32, scope_wb)
        scope_wb.close()
        scope_d2.close()
        scope_a = ExitStack()
        wa_raw = [sb(f"wa_raw{i}", [P, 2, 3, P], F32, scope_a) for i in range(2)]
        wa_hi = sb("wa_hi", [P, KC, 3 * P], F32R, scope_a)
        wa_lo = sb("wa_lo", [P, KC, 3 * P], F32R, scope_a)
        v_hi = [sb(f"v_hi{i}", [P, NB, P], F32R, scope_a) for i in range(2)]
        v_lo = [sb(f"v_lo{i}", [P, NB, P], F32R, scope_a) for i in range(2)]
        kT_hi = [sb(f"kT_hi{i}", [P, S], F32R, scope_a) for i in range(2)]
        kT_lo = [sb(f"kT_lo{i}", [P, S], F32R, scope_a) for i in range(2)]
        qT_hi = sb("qT_hi", [P, S], F32R, scope_a)
        qT_lo = sb("qT_lo", [P, S], F32R, scope_a)
        dist_a = sb("dist_a", [P, S], F32, scope_a)
        bias_a = [sb(f"bias_a{i}", [P, S], F32, scope_a) for i in range(2)]
        p0 = [sb(f"p0_{i}", [P, S], F32, scope_a) for i in range(2)]
        p1 = sb("p1", [P, S], F32, scope_a)
        wT_hi = sb("wT_hi", [P, NB, P], F32R, scope_a)
        wT_lo = sb("wT_lo", [P, NB, P], F32R, scope_a)
        qk2 = sb("qk2", [P, 2, 2 * P], F32, scope_a)
        sq_a = sb("sq_a", [P, 2 * P], F32, scope_a)
        oraw = sb("oraw", [P, NB, P], F32, scope_a)
        ojunk = sb("ojunk", [P, P], F32, scope_a)
        rstd_qk = sb("rstd_qk", [P, 8], F32, scope_a)
        rstd_o = sb("rstd_o", [P, NB], F32, scope_a)
        oss = sb("oss", [P, NB], F32, scope_a)
        ssum = [sb(f"ssum{i}", [P, 2, NB], F32, scope_a) for i in range(2)]
        s0sq = sb("s0sq", [P, NB], F32, scope_a)
        mx_a = sb("mx_a", [P, 2], F32, scope_a)
        nm_a = sb("nm_a", [P, 2], F32, scope_a)
        rcp_a = sb("rcp_a", [P, 1], F32, scope_a)
        coef_a = sb("coef_a", [P, 1], F32, scope_a)
        scope_a.close()
        scope_x = ExitStack()
        pad_x = sb("pad_x", [P, 6 * 256], F32, scope_x)
        x_tok = sb("x_tok", [P, NB, D], F32, scope_x)
        x_junk = sb("x_junk", [P, D], F32, scope_x)
        x_stage = [sb(f"x_stage{i}", [P, HALF], F32, scope_x) for i in range(2)]
        scope_x.close()
        scope_d.close()
        scope_b = ExitStack()
        kraw = sb("kraw", [P, NB, 256], F32, scope_b)
        vb_hi = sb("vb_hi", [P, NB, 256], F32R, scope_b)
        vb_lo = sb("vb_lo", [P, NB, 256], F32R, scope_b)
        kn = sb("kn", [P, NB, 2, HD], F32, scope_b)
        kTb_hi = sb("kTb_hi", [P, S], F32R, scope_b)
        kTb_lo = sb("kTb_lo", [P, S], F32R, scope_b)
        pb = [sb(f"pb{i}", [P, GRP, 256], F32, scope_b) for i in range(2)]
        wTb_hi = sb("wTb_hi", [P, 2, HALF], F32R, scope_b)
        wTb_lo = sb("wTb_lo", [P, 2, HALF], F32R, scope_b)
        qTb_hi = [sb(f"qTb_hi{i}", [P, 2, P], F32R, scope_b) for i in range(2)]
        qTb_lo = [sb(f"qTb_lo{i}", [P, 2, P], F32R, scope_b) for i in range(2)]
        scope_b.close()
        oT = xT

        score = [ctx.enter_context(nc.psum_tensor(f"score{i}", [P, 2 * HALF], F32)) for i in range(2)]
        proj = ctx.enter_context(nc.psum_tensor("proj", [P, HALF], F32))
        trb = [ctx.enter_context(nc.psum_tensor(f"trb{i}", [P, HALF], F32)) for i in range(2)]
        pv = ctx.enter_context(nc.psum_tensor("pv", [P, HALF], F32))
        bank = [[score[i][:, HALF * h:HALF * (h + 1)] for h in range(2)] for i in range(2)]

        x_dram = nc.dram_tensor("xT_dram", [P, KC, S], F32, kind="Internal").ap()

        const_in, made, made2, made3 = sem("const_in"), sem("made"), sem("made2"), sem("made3")
        small_mm, sinks_done, lam_exp = sem("small_mm"), sem("sinks_done"), sem("lam_exp")
        x_half_in = [sem(f"x_half_in{i}") for i in range(2)]
        x_tr, x_hi_done, x_staged, x_bank_free = sem("x_tr"), sem("x_hi_done"), sem("x_staged"), sem("x_bank_free")
        x_stored = [sem(f"x_stored{i}") for i in range(2)]
        row_stats, x_stat = sem("row_stats"), sem("x_stat")
        wa_in = [sem(f"wa_in{i}") for i in range(2)]
        wa_hi_done, wa_lo_done = sem("wa_hi_done"), sem("wa_lo_done")
        qkv_ready, qkv_free, qkv_copied, sq_done, red_done = (
            sem("qkv_ready"), sem("qkv_free"), sem("qkv_copied"), sem("sq_done"), sem("red_done"))
        qk_rstd, qk_normed, pair_hi, kT_done = sem("qk_rstd"), sem("qk_normed"), sem("pair_hi"), sem("kT_done")
        scores_ready, score_max, nm_ready, exp_done, mixed = (
            sem("scores_ready"), sem("score_max"), sem("nm_ready"), sem("exp_done"), sem("mixed"))
        tr_ready, tr_free = sem("tr_ready"), [sem(f"tr_free{i}") for i in range(2)]
        wT_hi_done, pv_ready, pv_free = sem("wT_hi_done"), sem("pv_ready"), sem("pv_free")
        o_rstd, o_normed, bias_ready = sem("o_rstd"), sem("o_normed"), sem("bias_ready")
        o_split_hi, o_split, x_back = sem("o_split_hi"), sem("o_split"), sem("x_back")
        w_in = [sem(f"w_in{i}") for i in range(2)]
        w_hi_done, w_lo_done, panel_half = sem("w_hi_done"), sem("w_lo_done"), sem("panel_half")
        bank_free = [[sem(f"bank_free{i}{h}") for h in range(2)] for i in range(2)]
        u_hi_done, u_sq_done, u_split = sem("u_hi_done"), sem("u_sq_done"), sem("u_split")
        x_added, b_hi_done, b_split, x_sq, ss_added = (
            sem("x_added"), sem("b_hi_done"), sem("b_split"), sem("x_sq"), sem("ss_added"))
        ss_sum, r2_ready, x_parked = sem("ss_sum"), sem("r2_ready"), sem("x_parked")
        wb_in, wb_hi_done, wb_lo_done = sem("wb_in"), sem("wb_hi_done"), sem("wb_lo_done")
        pb_ready, pb_free, sqb_done, redb_done = sem("pb_ready"), sem("pb_free"), sem("sqb_done"), sem("redb_done")
        vb_hi_done, rstdb, qb_normed, kn_ready = sem("vb_hi_done"), sem("rstdb"), sem("qb_normed"), sem("kn_ready")
        bm_ready, bm_free = [sem(f"bm_ready{i}") for i in range(2)], [sem(f"bm_free{i}") for i in range(2)]
        bm_hi = [sem(f"bm_hi{i}") for i in range(2)]
        qt_ready, qt_hi, qt_free = sem("qt_ready"), sem("qt_hi"), sem("qt_free")
        sb_ready, sb_max, nmb_ready, expb_done = sem("sb_ready"), sem("sb_max"), sem("nmb_ready"), sem("expb_done")
        pvb_ready, pvb_free, ot_ready, ot_free = sem("pvb_ready"), sem("pvb_free"), sem("ot_ready"), sem("ot_free")
        biasb_ready, pz = sem("biasb_ready"), sem("pz")
        out_tr, out_staged, out_bank = sem("out_tr"), sem("out_staged"), sem("out_bank")
        dve_passed, act_passed = sem("dve_passed"), sem("act_passed")
        out_done = [sem(f"out_done{i}") for i in range(2)]

        block = ctx.enter_context(nc.Block())

        def walk(eng, seg, run, before_down=None):
            first = seg * SEG

            def pairs(kind, half_start, quarter, lo, hi, **flags):
                def body(j):
                    for i in range(2):
                        run(kind, (half_start + j) * 2 + i, half_start + j, j * 2 + i, quarter, i, **flags)
                if hi - lo == 1:
                    body(lo)
                else:
                    with eng.Fori(lo, hi) as j:
                        body(j)

            def quarter_of(q, **flags):
                up = q * KC + (first + KC) // 2
                down = up + KC // 2
                n = KC // 2
                if flags.get("first"):
                    pairs("up", up, q, 0, 1, head=True, **flags)
                    pairs("up", up, q, 1, n, **flags)
                    if before_down:
                        before_down()
                    pairs("down", down, q, 0, 1, head=True, **flags)
                    pairs("down", down, q, 1, n, **flags)
                    return
                pairs("up", up, q, 0, n, **flags)
                if not flags.get("last"):
                    pairs("down", down, q, 0, n, **flags)
                    return
                pairs("down", down, q, 0, 1, head=True, **flags)
                pairs("down", down, q, 1, n - 1, **flags)
                pairs("down", down, q, n - 1, n, tail=True, **flags)

            pairs("wo", first // 2, 0, 0, KC // 2)
            quarter_of(0, first=True)
            with eng.Fori(1, QUARTERS - 1) as q:
                quarter_of(q)
            quarter_of(QUARTERS - 1, last=True)

        def chunk_of(t, c, half):
            cols = slice(HALF * half, HALF * (half + 1))
            if isinstance(c, int):
                return t[:, c, cols]
            return t[:, bass.ds(c, 1), cols].rearrange("p a n -> p (a n)")

        def one(t, c):
            return t[:, c:c + 1] if isinstance(c, int) else t[:, bass.ds(c, 1)]

        def run_heads(eng, head):
            head(-1, 1, False, False, True)
            head(0, 0, True, False, True)
            with eng.Fori(0, 3) as i:
                head(2 * i + 1, 1, True, True, True)
                head(2 * i + 2, 0, True, True, True)
            head(NH - 1, 1, True, True, False)

        def uses_a(h, attn, tail, qkv):
            if isinstance(h, int) and h == -1:
                k = 18
            elif isinstance(h, int) and h == 0:
                k = 3
            else:
                k = -1
            plan, _ = plan_a(k, attn, tail, qkv)
            return {key: (n % 2, h * 9 + n // 2, h * 18 + n) for key, n in plan.items()}

        def up_half(seg, quarter, chunk, half):
            return seg * 64 + quarter * 16 + chunk * 2 + half

        def out_index(chunk, half):
            return chunk * 2 + half

        def magic_rsqrt(dve, out, vec, n):
            v, sh, t = vec[:, 0:n], chain_s[:, 0:n], chain_t[:, 0:n]
            dve.drain()
            dve.tensor_scalar(sh, v.bitcast(I32), 1, None, ALU.logical_shift_right)
            dve.drain()
            dve.tensor_scalar(out.bitcast(I32), sh, -1.0, float(0x5F3759DF), ALU.mult, ALU.add)
            for i in range(3):
                dve.drain()
                dve.tensor_tensor(t, out, out, ALU.mult)
                dve.drain()
                dve.tensor_tensor(t, t, v, ALU.mult)
                dve.drain()
                dve.tensor_scalar(t, t, -0.5, 1.5, ALU.mult, ALU.add)
                dve.drain()
                last = dve.tensor_tensor(out, out, t, ALU.mult)
            return last

        def pair_of(s, par):
            if s == 0:
                return par, slice(6 * P, 8 * P)
            return 1 - par, slice((s - 2) * P, s * P)

        def score_cols(j, lo):
            first = HALF * (j % 2) + 256 * (j // 2)
            return score[0][:, first + lo:first + 256]

        def uses_b(g, lag, proj_on, which):
            if isinstance(g, int) and g == 0:
                plan, _ = plan_b(0, 0, list(which), False)
                return plan
            plan, _ = plan_b(-2, -2, list(which), True)
            return {k: (g * (8 if k[-1] == 0 else 9)) + n for k, n in plan.items()}

        last_uses = {("lag", 0, i): ((140 + i) % 2, (140 + i) // 2, 140 + i) for i in range(2)}
        last_uses.update({("o", i): ((142 + i) % 2, (142 + i) // 2, 142 + i) for i in range(2)})

        @block.sync
        def _(sp):
            def col(dst, src):
                sp.dma_start(dst, src, allow_slow_non_contiguous=True).then_inc(const_in, 16)

            for i, src in enumerate((io["attn_norm_g"][0], io["mlp_norm_g"][0], io["mlp_norm_g"][1],
                                     io["kv_norm_g"], io["attn_norm_g"][1])):
                if i == 0:
                    col(gains[:, i, :], src.rearrange("(c p) -> p c", p=P))
                    for half in range(2):
                        for b in range(4 * half, 4 * half + 4):
                            sp.dma_start(x_tok[:, b, :], io["x"][0, P * b:P * (b + 1), :]).then_inc(x_half_in[half], 16)
                else:
                    col(gains[:, i, :], src.rearrange("(c p) -> p c", p=P))
            for i, src in enumerate((io["a_q_norm_g"][0], io["a_k_norm_g"][0], io["b_q_norm_g"][0], io["kv_k_norm_g"])):
                for half in range(2):
                    col(heads64[HD * half:HD * (half + 1), i:i + 1], src.rearrange("(p a) -> p a", a=1))
            col(gsub[:, :], io["a_subln_g"][0].rearrange("(p a) -> p a", a=1))
            for i, name in enumerate(("a_lambda_q1", "a_lambda_k1", "a_lambda_q2", "a_lambda_k2")):
                col(lam_in[:, i:i + 1], io[name][0].rearrange("(p a) -> p a", a=1))
            col(sink_col[:, :], io["b_sinks"][0].rearrange("(p a) -> p a", a=1))

            wqkv = io["a_w_qkv"][0].rearrange("(k p) (t n) -> p k t n", p=P, t=3)

            def load_wa(hq, i):
                for t in range(3):
                    sp.dma_start(wa_raw[i % 2][:, :, t, :],
                                 wqkv[:, 2 * i:2 * i + 2, t, bass.ds(hq * P, P)]).then_inc(wa_in[i % 2], 16)

            for i in range(2):
                load_wa(0, i)
            for n in range(2 * KC):
                sp.wait_ge(x_staged, n + 1)
                sp.dma_start(x_dram[:, n % KC, HALF * (n // KC):HALF * (n // KC + 1)],
                             x_stage[n % 2][:, :]).then_inc(x_stored[n % 2], 16)
            for i in range(2, 4):
                sp.wait_ge(wa_lo_done, i - 1)
                load_wa(0, i)
            with sp.Fori(1, NH) as hq:
                for i in range(4):
                    sp.wait_ge(wa_lo_done, hq * 4 + (i - 1))
                    load_wa(hq, i)

            w_of = {
                "wo": (io["a_w_o"][0], io["b_w_o"][0]),
                "up": (io["mlp_w_up"][0], io["mlp_w_up"][1]),
                "down": (io["mlp_w_down"][0], io["mlp_w_down"][1]),
            }

            def segment(seg):
                def load(kind, panel, chunk, quarter, slot):
                    w = w_of[kind][seg].rearrange("(k p) n -> p k n", p=P)
                    if kind == "up":
                        src = w[:, :, bass.ds((quarter * KC + chunk) * P, P)]
                    elif kind == "wo":
                        src = w[:, :, bass.ds(chunk * P, P)]
                    else:
                        src = w[:, bass.ds(quarter * KC, KC), bass.ds(chunk * P, P)]
                    if not isinstance(panel, int) or panel >= 2:
                        sp.wait_ge(w_lo_done, panel - 1)
                    sp.dma_start(w_raw[slot][:, :, :], src).then_inc(w_in[slot], 16)

                if seg == 0:
                    sp.wait_ge(tr_ready, 144)
                    sp.wait_ge(x_stored[0], 16 * KC)
                    sp.wait_ge(x_stored[1], 16 * KC)
                else:
                    sp.wait_ge(ot_free, 32)
                    sp.wait_ge(x_parked, 16 * 2 * KC)
                first = seg * SEG
                for i in range(2):
                    load("wo", first + i, i, 0, i)
                for c in range(KC):
                    sp.wait_ge(o_split, seg * KC + c + 1)
                    sp.dma_start(xT[:, c, :], x_dram[:, c, :]).then_inc(x_back, 16)
                with sp.Fori(1, KC // 2) as j:
                    for i in range(2):
                        load("wo", j * 2 + (first + i), j * 2 + i, 0, i)
                with sp.Fori(0, QUARTERS) as q:
                    for kind, start in (("up", first + KC), ("down", first + 2 * KC)):
                        with sp.Fori(0, KC // 2) as j:
                            for i in range(2):
                                load(kind, q * (2 * KC) + j * 2 + (start + i), j * 2 + i, q, i)

            segment(0)
            sp.wait_ge(panel_half, 2 * SEG)
            wkv = io["w_kv"].rearrange("(k p) n -> p k n", p=P)
            wq = io["b_w_q"][0].rearrange("(k p) n -> p k n", p=P)
            for j in range(2):
                if j:
                    sp.wait_ge(wb_lo_done, KC * j)
                sp.dma_start(wb_raw[:, :, :], wkv[:, :, 256 * j:256 * (j + 1)]).then_inc(wb_in, 16)
            with sp.Fori(0, KVH) as g:
                sp.wait_ge(wb_lo_done, g * KC + 2 * KC)
                sp.dma_start(wb_raw[:, :, :], wq[:, :, bass.ds(g * 256, 256)]).then_inc(wb_in, 16)
            segment(1)

        @block.gpsimd
        def _(pool):
            pool.memset(ident[:, :], 0.0).then_inc(made, 1)
            pool.memset(ones[:, :], 1.0).then_inc(made, 1)
            for h in range(NH):
                pool.memset(slopes[:, h:h + 1], float(np.float32(2.0 ** (-8.0 * (h + 1) / NH))))
            for h in range(16):
                pool.memset(slopes[:, NH + h:NH + h + 1], float(np.float32(2.0 ** (-8.0 * (h + 1) / 16))))
            pool.iota(dist_a[:, :], [[-1, S]], base=S - P, channel_multiplier=1,
                      allow_small_or_imprecise_dtypes=True).then_inc(made, 1)
            pool.wait_ge(made, 3)
            pool.affine_select(out=ident[:, :], in_=ident[:, :], compare_op=ALU.not_equal, fill=1.0, base=0,
                               pattern=[[-1, P]], channel_multiplier=1).then_inc(made2, 1)

            def bias_of(h, par):
                if not isinstance(h, int) or h >= 2:
                    pool.wait_ge(score_max, h * 16 - 16)
                pool.tensor_tensor(bias_a[par][:, :], dist_a[:, :], one(slopes, h).to_broadcast([P, S]), ALU.mult)\
                    .then_inc(bias_ready, 1)

            def head(h, par, attn, tail, qkv):
                if qkv:
                    bias_of(h + 1, 1 - par)
                for s in range(NB):
                    if s == 1 and tail:
                        pool.wait_ge(o_rstd, h)
                        pool.tensor_tensor(oraw[:, :, :], oraw[:, :, :],
                                           rstd_o[:, :].unsqueeze(2).to_broadcast([P, NB, P]), ALU.mult)\
                            .then_inc(o_normed, 1)
                    if s % 2 == 1 and qkv:
                        pool.wait_ge(qk_rstd, h * 4 + 4 + s // 2 + 1)
                        v = qk2[:, :, :].rearrange("p a (b d) -> p (a b) d", d=HD)
                        pool.tensor_tensor(v, v, rstd_qk[:, :].unsqueeze(2).to_broadcast([P, 8, HD]), ALU.mult)\
                            .then_inc(qk_normed, 1)

            pool.wait_ge(made3, 1)
            run_heads(pool, head)
            pool.wait_ge(o_rstd, NH)
            pool.tensor_tensor(oraw[:, :, :], oraw[:, :, :],
                               rstd_o[:, :].unsqueeze(2).to_broadcast([P, NB, P]), ALU.mult).then_inc(o_normed, 1)

            def add_square(z, half, clears):
                pool.wait_ge(x_sq, z + 1)
                pool.wait_ge(ss_added, z + (clears - 1))
                sh = ss[:, HALF * half:HALF * (half + 1)]
                pool.tensor_tensor(sh, sh, e1[half][:, :], ALU.add).then_inc(ss_added, 1)

            def segment(seg):
                def run(kind, panel, use, chunk, quarter, slot, **flags):
                    for half in range(2):
                        if kind == "wo":
                            add_square(chunk * 2 + (32 * seg + half), half, 2 + 4 * seg)
                        elif kind == "up":
                            u = up_half(seg, quarter, chunk, half)
                            pool.wait_ge(bank_free[slot][half], use + 1)
                            if not isinstance(u, int) or u >= 2:
                                pool.wait_ge(u_split, u - 1)
                            if not isinstance(quarter, int) or quarter or seg:
                                pool.wait_ge(x_added, up_half(seg, quarter, 0, half) - 1)
                            pool.tensor_tensor(e2[half][:, :], e1[half][:, :], e1[half][:, :], ALU.mult)\
                                .then_inc(u_sq_done, 1)
                        else:
                            v = up_half(seg, quarter, chunk, half)
                            pool.wait_ge(bank_free[slot][half], use + 1)
                            x_c = chunk_of(xT, chunk, half)
                            if flags.get("last") and seg == 1:
                                if not flags.get("head") or slot:
                                    pool.wait_ge(out_tr, out_index(chunk, half) - 1)
                                pool.tensor_tensor(e1[half][:, :], x_c, e2[half][:, :], ALU.add).then_inc(x_added, 1)
                                continue
                            pool.tensor_tensor(x_c, x_c, e2[half][:, :], ALU.add).then_inc(x_added, 1)
                    if kind == "down" and flags.get("last") and seg == 0:
                        for half in range(2):
                            add_square(chunk * 2 + (16 + half), half, 4)

                def clear():
                    for half in range(2):
                        pool.memset(ss[:, HALF * half:HALF * (half + 1)], 0.0).then_inc(ss_added, 1)

                if seg == 0:
                    pool.wait_ge(tr_ready, 144)
                    clear()
                    walk(pool, seg, run, before_down=lambda: (pool.wait_ge(ss_sum, 2), clear()))
                else:
                    pool.wait_ge(ot_free, 32)
                    clear()
                    walk(pool, seg, run)

            segment(0)

            pool.wait_ge(panel_half, 2 * SEG)
            pool.wait_ge(ss_sum, 3)
            pool.wait_ge(u_split, 64)
            pool.iota(dist_b[:, :], [[-1, 256]], base=P, channel_multiplier=1,
                      allow_small_or_imprecise_dtypes=True).then_inc(made, 1)
            for i in range(2):
                pool.memset(pb[i][:, :, :], 0.0).then_inc(pz, 1)
            pool.wait_ge(made3, 2)

            def q_norm(t, par):
                pool.wait_ge(rstdb, t + NB + 1)
                pool.wait_ge(pb_free, t + 2 * NB + 1)
                v = qraw_b[par][:, :].rearrange("p (a d) -> p a d", d=HD)
                pool.tensor_tensor(v, v, rstd_q[par][:, :].unsqueeze(2).to_broadcast([P, GRP, HD]), ALU.mult)\
                    .then_inc(qb_normed, 1)

            def group(g, lag):
                if lag:
                    pool.wait_ge(sb_max, g * NB - (NB - 1))
                else:
                    pool.wait_ge(rstdb, NB)
                    pool.wait_ge(pb_free, NB)
                for d in range(2):
                    pool.tensor_tensor(kn[:, :, d, :], kraw[:, :, bass.ds(g * HD, HD)],
                                       rstd_k[:, :, bass.ds(g, 1)].to_broadcast([P, NB, HD]), ALU.mult)\
                        .then_inc(kn_ready, 1)
                for s in range(NB):
                    if s == 1:
                        if lag:
                            pool.wait_ge(sb_max, g * NB)
                        for j in range(GRP):
                            pool.tensor_tensor(bias_b[:, j, :], dist_b[:, :],
                                               one(slopes, g * GRP + (NH + j)).to_broadcast([P, 256]), ALU.mult)\
                                .then_inc(biasb_ready, 1)
                    q_norm(g * NB + s, s % 2)

            group(0, False)
            with pool.Fori(1, KVH) as g:
                group(g, True)
            segment(1)

        @block.scalar
        def _(act):
            def copy(out, in_, scale=1.0):
                return nc.scalar.activation(out, in_, ACT.Copy, scale=scale)

            act.wait_ge(const_in, 16 * CONSTS)
            for n in range(2 * KC):
                half, c = divmod(n, KC)
                act.wait_ge(x_tr, n + 1)
                ps = bank[n % 2][n // 2 % 2]
                copy(a_hi[:, c, HALF * half:HALF * (half + 1)], ps, gains[:, 0, c:c + 1]).then_inc(x_hi_done, 1)
                if n >= 2:
                    act.wait_ge(x_stored[n % 2], 16 * (n // 2))
                copy(x_stage[n % 2][:, :], ps).then_inc(x_staged, 1)
            act.wait_ge(small_mm, 1)
            nc.scalar.activation(lam_e[:, :], proj[:, 0:2], ACT.Exp).then_inc(lam_exp, 1)
            act.wait_ge(row_stats, 1)

            def wa_split(hq):
                if not isinstance(hq, int) or hq > 0:
                    act.wait_ge(qkv_ready, hq * NB)
                for i in range(4):
                    act.wait_ge(wa_in[i % 2], hq * 96 + 48 * (i // 2 + 1))
                    copy(wa_hi[:, 2 * i:2 * i + 2, :].rearrange("p k n -> p (k n)"),
                         wa_raw[i % 2][:, :, :, :].rearrange("p k t n -> p (k t n)")).then_inc(wa_hi_done, 1)

            def head(h, par, attn, tail, qkv):
                uses = uses_a(h, attn, tail, qkv)
                hq = h + 1
                for s in range(NB):
                    t = h * NB + s
                    lag = ("lag", s, 0) in uses
                    for i in range(2):
                        if ("lag", s, i) in uses:
                            b, _, n = uses["lag", s, i]
                            blocks = (s - 1) % NB + 1
                            cols = P * (min(4 * i + 4, blocks) - 4 * i)
                            act.wait_ge(tr_ready, n + 1)
                            copy(wT_hi[:, 4 * i:4 * i + cols // P, :].rearrange("p a n -> p (a n)"),
                                 trb[b][:, 0:cols]).then_inc(wT_hi_done, 1)
                    if s == 0 and qkv:
                        wa_split(hq)
                    if attn:
                        keys = P * (s + 1)
                        act.wait_ge(nm_ready, t + 1)
                        for c, p in ((0, p0[s % 2]), (1, p1)):
                            nc.scalar.activation(p[:, 0:keys], p[:, 0:keys], ACT.Exp, bias=nm_a[:, c:c + 1],
                                                 accum_out=ssum[par][:, c, s:s + 1]).then_inc(exp_done, 1)
                    if ("pair", s) in uses:
                        b, _, n = uses["pair", s]
                        kp, cols = pair_of(s, par)
                        act.wait_ge(tr_ready, n + 1)
                        copy(qT_hi[:, cols], trb[b][:, 0:256])
                        copy(kT_hi[kp][:, cols], trb[b][:, 256:512], heads64[:, 4:5]).then_inc(pair_hi, 1)
                    if qkv:
                        act.wait_ge(qkv_ready, t + NB + 1)
                        if s == 0 and tail:
                            act.wait_ge(pv_ready, h * NB)
                        copy(v_hi[1 - par][:, s, :], proj[:, 256:384], row_r[:, s:s + 1])
                        copy(qk2[:, s % 2, :], proj[:, 0:256]).then_inc(qkv_copied, 1)
                        if not isinstance(h, int) or h >= 0 or s:
                            act.wait_ge(red_done, t + NB)
                        act.wait_ge(qkv_copied, t + NB + 1)
                        nc.scalar.activation(sq_a[:, :], qk2[:, s % 2, :], ACT.Square).then_inc(sq_done, 1)
                    if s == 1 and tail:
                        evac_o(uses, h - 1)
                    if lag:
                        evac_pv(t - 1, (s - 1) % NB)

            def evac_o(uses, h):
                for i in range(2):
                    b, _, n = uses["o", i]
                    act.wait_ge(tr_ready, n + 1)
                    copy(chunk_of(oT, h, i), trb[b][:, :], gsub[:, 0:1]).then_inc(tr_free[b], 1)

            def evac_pv(t, s):
                act.wait_ge(pv_ready, t + 1)
                copy(oraw[:, s, :], pv[:, 0:P])
                nc.scalar.activation(ojunk[:, :], pv[:, 0:P], ACT.Square, accum_out=oss[:, s:s + 1])\
                    .then_inc(pv_free, 1)

            for half in range(2):
                act.wait_ge(x_stored[half], 16 * KC)
            run_heads(act, head)
            for i in range(2):
                b, _, n = last_uses["lag", 0, i]
                act.wait_ge(tr_ready, n + 1)
                copy(wT_hi[:, 4 * i:4 * i + 4, :].rearrange("p a n -> p (a n)"), trb[b][:, :]).then_inc(wT_hi_done, 1)
            evac_pv(NH * NB - 1, NB - 1)
            evac_o(last_uses, NH - 1)

            def split_panel(panel, use, slot):
                act.wait_ge(w_in[slot], use * 16 + 16)
                if not isinstance(panel, int) or panel >= 2:
                    act.wait_ge(panel_half, panel * 2 - 2)
                copy(w_hi[slot][:, :, :].rearrange("p k n -> p (k n)"),
                     w_raw[slot][:, :, :].rearrange("p k n -> p (k n)")).then_inc(w_hi_done, 1)

            def next_input(z, clears, chunk, half, gain):
                copy(chunk_of(b_hi, chunk, half), chunk_of(xT, chunk, half),
                     1.0 if gain is None else one(gains[:, gain, :], chunk)).then_inc(b_hi_done, 1)
                act.wait_ge(ss_added, z + (clears - 1))
                act.sem_inc(act_passed, 1)
                nc.scalar.activation(e1[half][:, :], chunk_of(xT, chunk, half), ACT.Square).then_inc(x_sq, 1)

            def segment(seg):
                def run(kind, panel, use, chunk, quarter, slot, **flags):
                    if not (flags.get("tail") and slot == 1):
                        split_panel(panel + 1, use + slot, 1 - slot)
                    for half in range(2):
                        if kind == "wo":
                            act.wait_ge(bank_free[slot][half], use + 1)
                            next_input(chunk * 2 + (32 * seg + half), 2 + 4 * seg, chunk, half, 1 + seg)
                        elif kind == "up":
                            u = up_half(seg, quarter, chunk, half)
                            act.wait_ge(panel_half, panel * 2 + half + 1)
                            if flags.get("first") and flags.get("head") and slot == 0:
                                act.wait_ge(ss_added, 18 + 36 * seg)
                            else:
                                act.wait_ge(u_sq_done, u - 1)
                            nc.scalar.activation(e1[half][:, :], bank[slot][half], ACT.Relu)\
                                .then_inc(bank_free[slot][half], 1)
                            act.wait_ge(bank_free[slot][half], use + 1)
                            nc.scalar.activation(chunk_of(a_hi, chunk, half), e1[half][:, :], ACT.Square)\
                                .then_inc(u_hi_done, 1)
                        elif flags.get("last") and seg == 0:
                            act.wait_ge(x_added, up_half(seg, quarter, chunk, half) + 1)
                            next_input(chunk * 2 + (16 + half), 4, chunk, half, None)
                            act.dma_start(
                                x_dram[:, bass.ds(chunk, 1), HALF * half:HALF * (half + 1)].rearrange("p a n -> p (a n)"),
                                chunk_of(xT, chunk, half)).then_inc(x_parked, 16)
                    if kind == "down" and flags.get("last") and seg == 1:
                        if slot or not flags.get("head"):
                            store_out(chunk - 1)
                    if flags.get("tail") and slot == 1 and seg == 1:
                        store_out(chunk)

                def store_out(chunk):
                    for half in range(2):
                        n = out_index(chunk, half)
                        act.wait_ge(out_tr, n + 1)
                        if not isinstance(n, int) or n >= 2:
                            act.wait_ge(out_done[half], chunk * 16)
                        stage = ss[:, HALF * half:HALF * (half + 1)]
                        copy(stage, (proj, pv)[half][:, :]).then_inc(out_staged, 1)
                        act.wait_ge(out_staged, n + 1)
                        act.dma_start(
                            io["out"][0].rearrange("(h b p) d -> p h b d", h=2, p=P)[:, half, :, bass.ds(chunk * P, P)],
                            stage.rearrange("p (b d) -> p b d", d=P)).then_inc(out_done[half], 16)

                for c in range(KC):
                    if seg == 0:
                        act.wait_ge(tr_free[0], 72)
                        act.wait_ge(tr_free[1], 72)
                    else:
                        act.wait_ge(ot_free, 32)
                    copy(a_hi[:, c, :], oT[:, c, :]).then_inc(o_split_hi, 1)
                    if c == 0:
                        split_panel(seg * SEG, seg * SEG // 2, 0)
                walk(act, seg, run)
                if seg == 1:
                    for half in range(2):
                        act.wait_ge(out_done[half], 16 * KC)

            segment(0)

            def wb_split(job, gain):
                act.wait_ge(wb_in, job * 16 + 16)
                if not isinstance(job, int) or job > 0:
                    act.wait_ge(pb_ready, job * NB)
                for k in range(KC):
                    copy(wb_hi[:, k, :], wb_raw[:, k, :], gains[:, gain, k:k + 1]).then_inc(wb_hi_done, 1)

            def raw_and_squares(n, dst, red):
                act.wait_ge(pb_ready, n + 1)
                if not isinstance(red, int) or red > 0:
                    act.wait_ge(redb_done, red)
                nc.scalar.activation(sq_b[:, :], proj[:, 0:256], ACT.Square).then_inc(sqb_done, 1)
                copy(dst, proj[:, 0:256]).then_inc(pb_free, 1)

            act.wait_ge(panel_half, 2 * SEG)
            act.wait_ge(ss_sum, 3)
            wb_split(0, 3)
            for s in range(NB):
                raw_and_squares(s, kraw[:, s, :], s)
            wb_split(1, 3)
            for s in range(NB):
                act.wait_ge(pb_ready, NB + s + 1)
                copy(vb_hi[:, s, :], proj[:, 0:256], row_r[:, s:s + 1]).then_inc(vb_hi_done, 1)

            def steps(g, lag, proj_on, which):
                uses = uses_b(g, lag, proj_on, which)
                for s in which:
                    t = g * NB + s
                    if proj_on:
                        if s == 0:
                            wb_split(g + 2, 4)
                        raw_and_squares(t + 2 * NB, qraw_b[s % 2][:, :], t + NB)
                    if (s >= 1 or lag) and (proj_on or s == 0):
                        act.wait_ge(qt_ready, t)
                        copy(qTb_hi[(s - 1) % 2][:, :, :].rearrange("p a n -> p (a n)"), score[1][:, 0:256])\
                            .then_inc(qt_hi, 1)
                    for b in range(2):
                        if ("p", s, b) in uses:
                            act.wait_ge(bm_ready[b], uses["p", s, b] + 1)
                            copy(wTb_hi[:, b, :], trb[b][:, :]).then_inc(bm_hi[b], 1)
                    if (s >= 1 or lag) and (proj_on or s == 0):
                        par, lo = (s - 1) % 2, (P if s == 1 else CH)
                        act.wait_ge(nmb_ready, t)
                        for j in range(GRP):
                            nc.scalar.activation(pb[par][:, j, lo:256], pb[par][:, j, lo:256], ACT.Exp,
                                                 bias=nm_b[par][:, j:j + 1], accum_out=sm_b[par][:, j:j + 1])
                        nc.scalar.activation(es_b[par][:, :], esin_b[par][:, :], ACT.Exp).then_inc(expb_done, 1)
                    if s >= 3 or lag:
                        act.wait_ge(ot_ready, t - 2)
                        o_t = (s - 3) % NB
                        g_o = g if s >= 3 else g - 1
                        dst = oT[:, bass.ds(g_o * 2, 2), P * o_t:P * (o_t + 1)]
                        copy(dst, score[1][:, HALF:HALF + 256].rearrange("p (a n) -> p a n", a=2)).then_inc(ot_free, 1)
                    if ("k", 0) in uses and s == 0:
                        for b in range(2):
                            act.wait_ge(bm_ready[b], uses["k", b] + 1)
                            copy(kTb_hi[:, HALF * b:HALF * (b + 1)], trb[b][:, :], heads64[:, 5:6])\
                                .then_inc(bm_hi[b], 1)

            act.wait_ge(x_parked, 16 * 2 * KC)
            act.wait_ge(b_split, 32)
            act.wait_ge(pz, 2)
            steps(0, False, True, range(NB))
            with act.Fori(1, KVH) as g:
                steps(g, True, True, range(NB))
            steps(KVH, True, False, range(3))
            segment(1)

        @block.vector
        def _(dve):
            def low(out, full, hi, scale=None):
                if scale is None:
                    return nc.vector.tensor_tensor(out, full, hi.bitcast(F32), ALU.subtract)
                return nc.vector.scalar_tensor_tensor(out=out, in0=full, scalar=scale, in1=hi.bitcast(F32),
                                                      op0=ALU.mult, op1=ALU.subtract)

            def neg_abs(dist, masks):
                junk = x_junk[:, :] if dist is dist_a else sq_b[:, :]
                nc.vector.tensor_scalar(junk, dist[:, :], -1.0, None, ALU.mult)
                dve.drain()
                nc.vector.tensor_tensor(dist[:, :], dist[:, :], junk, ALU.min)
                for rows, cols in masks:
                    dve.drain()
                    last = nc.vector.memset(dist[rows, cols], MASK)
                return last

            dve.wait_ge(const_in, 16 * CONSTS)
            dve.wait_ge(made2, 1)
            nc.vector.tensor_tensor(lam_pr[:, 0:1], lam_in[:, 0:1], lam_in[:, 1:2], ALU.mult)
            nc.vector.tensor_tensor(lam_pr[:, 1:2], lam_in[:, 2:3], lam_in[:, 3:4], ALU.mult)
            nc.vector.tensor_scalar(sink_dg[:, :], ident[0:16, 0:16], sink_col[:, 0:1], None, ALU.mult)
            for i in range(2):
                nc.vector.scalar_tensor_tensor(out=heads64[:, 4 + i:5 + i], in0=heads64[:, 2 * i:2 * i + 1],
                                               scalar=HD ** -0.5, in1=heads64[:, 2 * i + 1:2 * i + 2],
                                               op0=ALU.mult, op1=ALU.mult)
            nc.vector.tensor_scalar(gsub[:, :], gsub[:, :], 1.0 - LAM0, None, ALU.mult).then_inc(sinks_done, 1)

            for n in range(2 * KC):
                half, c = divmod(n, KC)
                cols = slice(HALF * half, HALF * (half + 1))
                dve.wait_ge(x_hi_done, n + 1)
                dve.wait_ge(x_staged, n + 1)
                low(a_lo[:, c, cols], bank[n % 2][n // 2 % 2], a_hi[:, c, cols], gains[:, 0, c:c + 1])\
                    .then_inc(x_bank_free, 1)
                if c % 2 == 0:
                    b = n // 2
                    dve.wait_ge(x_half_in[half], 64)
                    if n:
                        dve.drain()
                    nc.vector.tensor_tensor_reduce(out=x_junk[:, :], in0=x_tok[:, b, :], in1=x_tok[:, b, :],
                                                   scale=1.0, scalar=0.0, op0=ALU.mult, op1=ALU.add,
                                                   accum_out=msq[:, b:b + 1])

            def row_factors():
                dve.drain()
                nc.vector.tensor_scalar(chain_v[:, 0:NB], msq[:, :], 1.0 / D, EPS, ALU.mult, ALU.add)
                magic_rsqrt(nc.vector, row_r[:, :], chain_v, NB)
                return nc.vector.tensor_scalar(msq[:, :], chain_v[:, 0:NB], EPS, None, ALU.mult)

            row_factors()
            dve.drain()
            neg_abs(dist_a, [(slice(0, CH), slice(S - CH, S))]).then_inc(made3, 1)
            dve.wait_ge(lam_exp, 1)
            nc.vector.tensor_copy(sinks[:, :], proj[:, 16:32])
            nc.vector.tensor_tensor(neg_lam[:, :], lam_e[:, 1:2], lam_e[:, 0:1], ALU.subtract)
            dve.drain()
            nc.vector.tensor_scalar(neg_lam[:, :], neg_lam[:, :], -LAM0, None, ALU.add)
            dve.drain().then_inc(row_stats, 1)

            def head(h, par, attn, tail, qkv):
                uses = uses_a(h, attn, tail, qkv)
                hq = h + 1
                for s in range(NB):
                    t = h * NB + s
                    keys = P * (s + 1)
                    if attn:
                        if s == 0:
                            dve.wait_ge(bias_ready, h + 1)
                        for c, p in ((0, p0[s % 2]), (1, p1)):
                            if c and not qkv:
                                dve.wait_ge(mixed, t)
                            dve.wait_ge(scores_ready, t * 2 + c + 1)
                            dve.sem_inc(dve_passed, 1)
                            nc.vector.tensor_tensor_reduce(
                                out=p[:, 0:keys], in0=score[c][:, 0:keys], in1=bias_a[par][:, S - keys:S],
                                scale=1.0, scalar=LOWEST, op0=ALU.add, op1=ALU.max,
                                accum_out=mx_a[:, c:c + 1]).then_inc(score_max, 1)
                        dve.wait_ge(score_max, t * 2 + 2)
                        nc.vector.tensor_scalar(nm_a[:, :], mx_a[:, :], -1.0, None, ALU.mult).then_inc(nm_ready, 1)
                    for i in range(2):
                        if ("lag", s, i) in uses:
                            low_wT(uses["lag", s, i], i, (s - 1) % NB, wt_use(h, s, i))
                    if s == 1 and tail:
                        o_factors(h, 1 - par)
                    if s == 0 and qkv:
                        for i in range(4):
                            dve.wait_ge(wa_hi_done, hq * 4 + i + 1)
                            low(wa_lo[:, 2 * i:2 * i + 2, :].rearrange("p k n -> p (k n)"),
                                wa_raw[i % 2][:, :, :, :].rearrange("p k t n -> p (k t n)"),
                                wa_hi[:, 2 * i:2 * i + 2, :].rearrange("p k n -> p (k n)")).then_inc(wa_lo_done, 1)
                    if ("pair", s) in uses:
                        b, _, n = uses["pair", s]
                        kp, cols = pair_of(s, par)
                        dve.wait_ge(pair_hi, (h * 4 + 4 + s // 2) if s else hq * 4)
                        low(kT_lo[kp][:, cols], trb[b][:, 256:512], kT_hi[kp][:, cols], heads64[:, 4:5])\
                            .then_inc(kT_done, 1)
                        low(qT_lo[:, cols], trb[b][:, 0:256], qT_hi[:, cols]).then_inc(tr_free[b], 1)
                    if attn:
                        dve.wait_ge(exp_done, t * 2 + 2)
                        nc.vector.reciprocal(rcp_a[:, :], ssum[par][:, 1, s:s + 1])
                        dve.drain()
                        nc.vector.scalar_tensor_tensor(out=coef_a[:, :], in0=ssum[par][:, 0, s:s + 1],
                                                       scalar=neg_lam[:, 0:1], in1=rcp_a[:, :],
                                                       op0=ALU.mult, op1=ALU.mult)
                        dve.drain()
                        p = p0[s % 2][:, 0:keys]
                        nc.vector.scalar_tensor_tensor(out=p, in0=p1[:, 0:keys], scalar=coef_a[:, 0:1], in1=p,
                                                       op0=ALU.mult, op1=ALU.add).then_inc(mixed, 1)
                    if qkv:
                        dve.wait_ge(qkv_copied, t + NB + 1)
                        low(v_lo[1 - par][:, s, :], proj[:, 256:384], v_hi[1 - par][:, s, :], row_r[:, s:s + 1])\
                            .then_inc(qkv_free, 1)
                        dve.wait_ge(sq_done, t + NB + 1)
                        m = stat_m[:, 4 * (s % 2):4 * (s % 2) + 4]
                        nc.vector.tensor_reduce(m, sq_a[:, :].rearrange("p (a d) -> p a d", d=HD), AX_X, ALU.add)\
                            .then_inc(red_done, 1)
                        if s % 2 and (not isinstance(h, int) or h >= 0 or s > 1):
                            dve.wait_ge(qk_normed, hq * 4 + s // 2)
                        dve.wait_ge(red_done, t + NB + 1)
                        nc.vector.tensor_scalar(chain_q[:, 4 * (s % 2):4 * (s % 2) + 4], m, 1.0 / HD, msq[:, s:s + 1],
                                                ALU.mult, ALU.add)
                        if s % 2:
                            magic_rsqrt(nc.vector, rstd_qk[:, :], chain_q, 8).then_inc(qk_rstd, 1)

            def low_wT(use, i, block_s, wt):
                b, _, n = use
                cols = P * (min(4 * i + 4, block_s + 1) - 4 * i)
                view = lambda w: w[:, 4 * i:4 * i + cols // P, :].rearrange("p a n -> p (a n)")
                dve.wait_ge(wT_hi_done, wt + 1)
                low(view(wT_lo), trb[b][:, 0:cols], view(wT_hi)).then_inc(tr_free[b], 1)

            def o_factors(done, par):
                dve.wait_ge(pv_free, done * NB)
                s0 = ssum[par][:, 0, :]
                nc.vector.tensor_tensor(s0sq[:, :], s0, s0, ALU.mult)
                nc.vector.tensor_scalar(chain_v[:, 0:NB], oss[:, :], 1.0 / P, None, ALU.mult)
                dve.drain()
                nc.vector.scalar_tensor_tensor(out=chain_v[:, 0:NB], in0=s0sq[:, :], scalar=EPS,
                                               in1=chain_v[:, 0:NB], op0=ALU.mult, op1=ALU.add)
                magic_rsqrt(nc.vector, rstd_o[:, :], chain_v, NB).then_inc(o_rstd, 1)

            def wt_use(h, s, i):
                block_s = (s - 1) % NB
                before = sum(lag_banks(x) for x in range(block_s))
                return (h - 1 if s == 0 else h) * 12 + before + i

            run_heads(dve, head)
            for i in range(2):
                low_wT(last_uses["lag", 0, i], i, NB - 1, wt_use(NH, 0, i))
            o_factors(NH, 1)

            def split_panel(panel, use, slot):
                dve.wait_ge(w_hi_done, panel + 1)
                low(w_lo[slot][:, :, :].rearrange("p k n -> p (k n)"),
                    w_raw[slot][:, :, :].rearrange("p k n -> p (k n)"),
                    w_hi[slot][:, :, :].rearrange("p k n -> p (k n)")).then_inc(w_lo_done, 1)

            def segment(seg):
                def run(kind, panel, use, chunk, quarter, slot, **flags):
                    if not (flags.get("tail") and slot == 1):
                        split_panel(panel + 1, use + slot, 1 - slot)
                    for half in range(2):
                        if kind == "wo":
                            dve.wait_ge(panel_half, panel * 2 + half + 1)
                            x_c = chunk_of(xT, chunk, half)
                            nc.vector.tensor_tensor(x_c, bank[slot][half], x_c, ALU.add)\
                                .then_inc(bank_free[slot][half], 1)
                        elif kind == "up":
                            u = up_half(seg, quarter, chunk, half)
                            dve.wait_ge(u_hi_done, u + 1)
                            dve.wait_ge(u_sq_done, u + 1)
                            low(chunk_of(a_lo, chunk, half), e2[half][:, :], chunk_of(a_hi, chunk, half))\
                                .then_inc(u_split, 1)
                        else:
                            v = up_half(seg, quarter, chunk, half)
                            dve.wait_ge(panel_half, panel * 2 + half + 1)
                            if not isinstance(v, int) or v >= 2:
                                dve.wait_ge(x_added, v - 1)
                            nc.vector.tensor_tensor(e2[half][:, :], bank[slot][half],
                                                    r2[:, HALF * half:HALF * (half + 1)], ALU.mult)\
                                .then_inc(bank_free[slot][half], 1)
                    for half in range(2):
                        if kind == "wo":
                            dve.wait_ge(b_hi_done, chunk * 2 + (32 * seg + half + 1))
                            low(chunk_of(b_lo, chunk, half), chunk_of(xT, chunk, half), chunk_of(b_hi, chunk, half),
                                one(gains[:, 1 + seg, :], chunk)).then_inc(b_split, 1)
                        if kind == "down" and flags.get("last") and seg == 0:
                            dve.wait_ge(b_hi_done, chunk * 2 + (16 + half + 1))
                            low(chunk_of(b_lo, chunk, half), chunk_of(xT, chunk, half), chunk_of(b_hi, chunk, half))\
                                .then_inc(b_split, 1)

                def mlp_factor():
                    for half in range(2):
                        dve.wait_ge(ss_sum, 3 * seg + half + 1)
                        cols = slice(HALF * half, HALF * (half + 1))
                        nc.vector.tensor_scalar(r2[:, cols], (proj, pv)[half][:, :], 1.0 / D, EPS, ALU.mult, ALU.add)
                        dve.drain()
                        nc.vector.reciprocal(r2[:, cols], r2[:, cols])
                    dve.drain().then_inc(r2_ready, 1)

                for c in range(KC):
                    dve.wait_ge(o_split_hi, seg * KC + c + 1)
                    low(a_lo[:, c, :], oT[:, c, :], a_hi[:, c, :]).then_inc(o_split, 1)
                    if c == 0:
                        split_panel(seg * SEG, seg * SEG // 2, 0)
                dve.wait_ge(x_back, 16 * KC * (seg + 1))
                walk(dve, seg, run, before_down=mlp_factor)

            segment(0)

            dve.wait_ge(panel_half, 2 * SEG)
            dve.wait_ge(ss_sum, 3)
            nc.vector.tensor_copy(msq[:, :], proj[:, 0:NB])
            row_factors()
            dve.drain().then_inc(row_stats, 1)
            dve.wait_ge(made, 4)
            dve.drain()
            neg_abs(dist_b, [(slice(0, CH), slice(256 - CH, 256)), (slice(CH, P), slice(0, P))]).then_inc(made3, 1)

            def wb_split(job, gain):
                for k in range(KC):
                    dve.wait_ge(wb_hi_done, job * KC + k + 1)
                    low(wb_lo[:, k, :], wb_raw[:, k, :], wb_hi[:, k, :], gains[:, gain, k:k + 1])\
                        .then_inc(wb_lo_done, 1)

            def norms(n, s, out):
                dve.wait_ge(sqb_done, n + 1)
                nc.vector.tensor_reduce(stat_m[:, 0:4], sq_b[:, :].rearrange("p (a d) -> p a d", d=HD), AX_X,
                                        ALU.add).then_inc(redb_done, 1)
                dve.wait_ge(redb_done, n + 1)
                nc.vector.tensor_scalar(chain_v[:, 0:4], stat_m[:, 0:4], 1.0 / HD, msq[:, s:s + 1], ALU.mult, ALU.add)
                magic_rsqrt(nc.vector, out, chain_v, 4).then_inc(rstdb, 1)

            wb_split(0, 3)
            for s in range(NB):
                norms(s, s, rstd_k[:, s, :])
            wb_split(1, 3)
            for s in range(NB):
                dve.wait_ge(vb_hi_done, s + 1)
                low(vb_lo[:, s, :], proj[:, 0:256], vb_hi[:, s, :], row_r[:, s:s + 1]).then_inc(pb_free, 1)

            def steps(g, lag, proj_on, which):
                uses = uses_b(g, lag, proj_on, which)
                for s in which:
                    t = g * NB + s
                    prev = (s >= 1 or lag) and (proj_on or s == 0)
                    if proj_on and s == 0:
                        wb_split(g + 2, 4)
                    if prev:
                        par = (s - 1) % 2
                        dve.wait_ge(qt_hi, t)
                        low(qTb_lo[par][:, :, :].rearrange("p a n -> p (a n)"), score[1][:, 0:256],
                            qTb_hi[par][:, :, :].rearrange("p a n -> p (a n)")).then_inc(qt_free, 1)
                    for b in range(2):
                        if ("p", s, b) in uses:
                            dve.wait_ge(bm_hi[b], uses["p", s, b] + 1)
                            low(wTb_lo[:, b, :], trb[b][:, :], wTb_hi[:, b, :]).then_inc(bm_free[b], 1)
                    if proj_on:
                        norms(t + NB, s, rstd_q[s % 2][:, :])
                    if prev:
                        lo = P if s == 1 else CH
                        g_p = g if s else g - 1
                        dve.wait_ge(sb_ready, t)
                        if s == 1:
                            dve.wait_ge(biasb_ready, g * GRP + GRP)
                        dve.sem_inc(dve_passed, 1)
                        for j in range(GRP):
                            nc.vector.tensor_tensor_reduce(
                                out=pb[par][:, j, lo:256], in0=score_cols(j, lo),
                                in1=bias_b[:, j, lo:256], scale=1.0, scalar=LOWEST, op0=ALU.add, op1=ALU.max,
                                accum_out=mx_b[:, j:j + 1])
                        dve.drain().then_inc(sb_max, 1)
                        sk = sinks[:, bass.ds(g_p * GRP, GRP)]
                        nc.vector.tensor_tensor(mx_b[:, :], mx_b[:, :], sk, ALU.max)
                        dve.drain()
                        nc.vector.tensor_tensor(esin_b[par][:, :], sk, mx_b[:, :], ALU.subtract)
                        nc.vector.tensor_scalar(nm_b[par][:, :], mx_b[:, :], -1.0, None, ALU.mult)\
                            .then_inc(nmb_ready, 1)
                    if (s >= 2 or lag) and (proj_on or s < 2):
                        par = s % 2
                        dve.wait_ge(expb_done, t - 1)
                        nc.vector.tensor_tensor(den_b[:, :], sm_b[par][:, :], es_b[par][:, :], ALU.add)
                        dve.drain()
                        nc.vector.reciprocal(rc_b[:, :], den_b[:, :])
                        dve.drain()
                        dve.wait_ge(pvb_ready, t - 1)
                        nc.vector.tensor_tensor(osb[par][:, :, :], pv[:, 0:256].rearrange("p (a d) -> p a d", d=HD),
                                                rc_b[:, :].unsqueeze(2).to_broadcast([P, GRP, HD]), ALU.mult)\
                            .then_inc(pvb_free, 1)
                    if ("k", 0) in uses and s == 0:
                        for b in range(2):
                            dve.wait_ge(bm_hi[b], uses["k", b] + 1)
                            low(kTb_lo[:, HALF * b:HALF * (b + 1)], trb[b][:, :], kTb_hi[:, HALF * b:HALF * (b + 1)],
                                heads64[:, 5:6]).then_inc(bm_free[b], 1)

            dve.wait_ge(pz, 2)
            steps(0, False, True, range(NB))
            with dve.Fori(1, KVH) as g:
                steps(g, True, True, range(NB))
            steps(KVH, True, False, range(3))
            segment(1)


        @block.tensor
        def _(pe):
            def mm(out, a, b, start, stop, **kw):
                return nc.tensor.matmul(out, a, b, start=start, stop=stop, **kw)

            def three(out, a, b, start, stop):
                mm(out, a[0], b[0], start, False)
                mm(out, a[0], b[1], False, False)
                return mm(out, a[1], b[0], False, stop)

            pe.wait_ge(made2, 1)
            for n in range(2 * KC):
                half, c = divmod(n, KC)
                if c == 0:
                    pe.wait_ge(x_half_in[half], 64)
                if n >= 4:
                    pe.wait_ge(x_bank_free, n - 3)
                for b in range(4):
                    last = nc.tensor.transpose(bank[n % 2][n // 2 % 2][:, P * b:P * (b + 1)],
                                               x_tok[:, 4 * half + b, P * c:P * (c + 1)], ident[:, :])
                last.then_inc(x_tr, 1)
            pe.wait_ge(sinks_done, 1)
            mm(proj[:, 0:2], ones[0:HD, :], lam_pr[:, :], True, True)
            mm(proj[:, 16:32], ones[0:16, :], sink_dg[:, :], True, True).then_inc(small_mm, 1)
            pe.wait_ge(row_stats, 1)

            def bank_for(b, before):
                if not isinstance(before, int) or before > 0:
                    pe.wait_ge(tr_free[b], before)

            def transpose_weights(uses, s, block_s, tw):
                pe.wait_ge(mixed, tw + 1)
                for i in range(lag_banks(block_s)):
                    b, before, n = uses["lag", s, i]
                    bank_for(b, before)
                    for kc in range(4 * i, min(4 * i + 4, block_s + 1)):
                        last = nc.tensor.transpose(trb[b][:, P * (kc - 4 * i):P * (kc - 4 * i + 1)],
                                                   p0[block_s % 2][:, P * kc:P * (kc + 1)], ident[:, :])
                    last.then_inc(tr_ready, 1)

            def values(uses, s, block_s, tw, vp):
                for i in range(lag_banks(block_s)):
                    b, before, _ = uses["lag", s, i]
                    pe.wait_ge(tr_free[b], before + 1)
                if not isinstance(tw, int) or tw > 0:
                    pe.wait_ge(pv_free, tw)
                for kc in range(block_s + 1):
                    last = three(pv[:, 0:P], (wT_hi[:, kc, :], wT_lo[:, kc, :]),
                                 (v_hi[vp][:, kc, :], v_lo[vp][:, kc, :]), kc == 0, kc == block_s)
                last.then_inc(pv_ready, 1)

            def transpose_outputs(uses, done):
                pe.wait_ge(o_normed, done)
                for i in range(2):
                    b, before, _ = uses["o", i]
                    bank_for(b, before)
                    for s in range(4):
                        last = nc.tensor.transpose(trb[b][:, P * s:P * (s + 1)], oraw[:, 4 * i + s, :], ident[:, :])
                    last.then_inc(tr_ready, 1)

            def head(h, par, attn, tail, qkv):
                uses = uses_a(h, attn, tail, qkv)
                for s in range(NB):
                    t = h * NB + s
                    if attn:
                        if s % 2 == 0:
                            pe.wait_ge(kT_done, h * 4 + s // 2 + 1)
                        for c in range(2):
                            rows = slice(HD * c, HD * (c + 1))
                            if not isinstance(h, int) or h or s:
                                pe.wait_ge(score_max, t * 2 + c - 1)
                            for k0 in range(0, P * (s + 1), HALF):
                                k1 = min(k0 + HALF, P * (s + 1))
                                q = slice(P * s, P * (s + 1))
                                last = three(score[c][:, k0:k1], (qT_hi[rows, q], qT_lo[rows, q]),
                                             (kT_hi[par][rows, k0:k1], kT_lo[par][rows, k0:k1]), True, True)
                            last.then_inc(scores_ready, 1)
                    lag = ("lag", s, 0) in uses
                    if lag:
                        transpose_weights(uses, s, (s - 1) % NB, t - 1)
                    if ("pair", s) in uses:
                        b, before, _ = uses["pair", s]
                        pe.wait_ge(qk_normed, (h * 4 + 4 + s // 2) if s else h * 4 + 4)
                        bank_for(b, before)
                        for i in range(4):
                            last = nc.tensor.transpose(trb[b][:, P * i:P * (i + 1)],
                                                       qk2[:, i % 2, P * (i // 2):P * (i // 2 + 1)], ident[:, :])
                        last.then_inc(tr_ready, 1)
                    if qkv:
                        if not isinstance(h, int) or h >= 0 or s:
                            pe.wait_ge(qkv_free, t + NB)
                        for k in range(KC):
                            if s == 0 and k % 2 == 0:
                                pe.wait_ge(wa_lo_done, h * 4 + 4 + k // 2 + 1)
                            tok = slice(P * s, P * (s + 1))
                            last = three(proj[:, 0:384], (a_hi[:, k, tok], a_lo[:, k, tok]),
                                         (wa_hi[:, k, :], wa_lo[:, k, :]), k == 0, k == KC - 1)
                        last.then_inc(qkv_ready, 1)
                    if s == 1 and tail:
                        transpose_outputs(uses, h)
                    if lag:
                        values(uses, s, (s - 1) % NB, t - 1, par if s else 1 - par)

            run_heads(pe, head)
            transpose_weights(last_uses, 0, NB - 1, NH * NB - 1)
            values(last_uses, 0, NB - 1, NH * NB - 1, 1)
            transpose_outputs(last_uses, NH)

            def segment(seg):
                def run(kind, panel, use, chunk, quarter, slot, **flags):
                    x_hi, x_lo = (b_hi, b_lo) if kind == "up" else (a_hi, a_lo)
                    pe.wait_ge(w_lo_done, panel + 1)
                    for half in range(2):
                        if not isinstance(panel, int) or panel >= 2:
                            pe.wait_ge(bank_free[slot][half], use)
                    for k in range(KC):
                        if kind == "wo":
                            pe.wait_ge(o_split, seg * KC + k + 1)
                        if kind == "up" and flags.get("first"):
                            pe.wait_ge(b_split, 32 * seg + 2 * k + 2)
                        if kind == "down" and k in (0, 6, 7):
                            pe.wait_ge(u_split, seg * 64 + quarter * 16 + (12 if k == 0 else 2 * k + 2))
                        w_h, w_l = w_hi[slot][:, k, :], w_lo[slot][:, k, :]
                        first, last = k == 0, k == KC - 1
                        out = bank[slot]
                        xs = [(x_hi[:, k, HALF * i:HALF * (i + 1)], x_lo[:, k, HALF * i:HALF * (i + 1)])
                              for i in range(2)]
                        if last:
                            for i in range(2):
                                three(out[i], (w_h, w_l), xs[i], False, True).then_inc(panel_half, 1)
                            continue
                        for i in range(2):
                            mm(out[i], w_h, xs[i][0], first, False)
                            mm(out[i], w_h, xs[i][1], False, False)
                        for i in range(2):
                            mm(out[i], w_l, xs[i][0], False, False)
                    if kind == "down" and flags.get("last") and seg == 1:
                        if slot or not flags.get("head"):
                            transpose_out(chunk - 1)
                        if flags.get("tail") and slot:
                            transpose_out(chunk)

                def transpose_out(chunk):
                    for half in range(2):
                        n = out_index(chunk, half)
                        pe.wait_ge(x_added, 64 + 48 + n + 1)
                        if not isinstance(n, int) or n >= 2:
                            pe.wait_ge(out_staged, n - 1)
                        for b in range(4):
                            last = nc.tensor.transpose((proj, pv)[half][:, P * b:P * (b + 1)],
                                                       e1[half][:, P * b:P * (b + 1)], ident[:, :])
                        last.then_inc(out_tr, 1)

                def sum_squares():
                    pe.wait_ge(ss_added, 18 + 36 * seg)
                    for half in range(2):
                        mm((proj, pv)[half][:, :], ones[:, :], ss[:, HALF * half:HALF * (half + 1)], True, True)\
                            .then_inc(ss_sum, 1)

                walk(pe, seg, run, before_down=sum_squares)

            segment(0)

            pe.wait_ge(ss_added, 36)
            pe.wait_ge(r2_ready, 1)
            for b in range(NB):
                last = mm(proj[:, b:b + 1], ss[:, P * b:P * (b + 1)], ones[:, 0:1], True, True)
            last.then_inc(ss_sum, 1)
            pe.wait_ge(row_stats, 2)

            def project(job, s):
                n = job * NB + s
                if not isinstance(job, int) or n > 0:
                    pe.wait_ge(pb_free, n)
                for k in range(KC):
                    if s == 0:
                        pe.wait_ge(wb_lo_done, job * KC + k + 1)
                        if isinstance(job, int) and job == 0:
                            pe.wait_ge(b_split, 16 + 2 * k + 2)
                    tok = slice(P * s, P * (s + 1))
                    last = three(proj[:, 0:256], (b_hi[:, k, tok], b_lo[:, k, tok]),
                                 (wb_hi[:, k, :], wb_lo[:, k, :]), k == 0, k == KC - 1)
                last.then_inc(pb_ready, 1)

            for job in range(2):
                for s in range(NB):
                    project(job, s)

            def steps(g, lag, proj_on, which):
                uses = uses_b(g, lag, proj_on, which)
                for s in which:
                    t = g * NB + s
                    prev = (s >= 1 or lag) and (proj_on or s == 0)
                    if proj_on:
                        project(g + 2, s)
                    if prev:
                        par = (s - 1) % 2
                        pe.wait_ge(qb_normed, t)
                        if not isinstance(g, int) or t >= 2:
                            pe.wait_ge(qt_free, t - 1)
                        for a in range(2):
                            last = nc.tensor.transpose(score[1][:, P * a:P * (a + 1)],
                                                       qraw_b[par][:, P * a:P * (a + 1)], ident[:, :])
                        last.then_inc(qt_ready, 1)
                    if (s >= 2 or lag) and (proj_on or s < 2):
                        pe.wait_ge(expb_done, t - 1)
                        for b in range(2):
                            if ("p", s, b) not in uses:
                                continue
                            before = uses["p", s, b]
                            if not isinstance(before, int) or before > 0:
                                pe.wait_ge(bm_free[b], before)
                            for j in range(GRP):
                                last = nc.tensor.transpose(trb[b][:, P * j:P * (j + 1)],
                                                           pb[s % 2][:, j, P * b:P * (b + 1)], ident[:, :])
                            last.then_inc(bm_ready[b], 1)
                    if prev:
                        par, blk = (s - 1) % 2, (s - 1) % NB
                        pe.wait_ge(qt_free, t)
                        if not isinstance(g, int) or t >= 2:
                            pe.wait_ge(sb_max, t - 1)
                        if s == 1:
                            for b in range(2):
                                pe.wait_ge(bm_free[b], uses["k", b] + 1)
                        lo = P if blk == 0 else CH
                        keys = slice(P * (blk - 1) + lo, P * (blk + 1))
                        for j in range(GRP):
                            rows = slice(HD * (j % 2), HD * (j % 2 + 1))
                            last = three(score_cols(j, lo),
                                         (qTb_hi[par][rows, j // 2, :], qTb_lo[par][rows, j // 2, :]),
                                         (kTb_hi[rows, keys], kTb_lo[rows, keys]), True, True)
                        last.then_inc(sb_ready, 1)
                    if (s >= 2 or lag) and (proj_on or s < 2):
                        blk = (s - 2) % NB
                        g_v = g if s >= 2 else g - 1
                        if not isinstance(g, int) or t > 2:
                            pe.wait_ge(pvb_free, t - 2)
                        for b in range(2):
                            if ("p", s, b) in uses:
                                pe.wait_ge(bm_free[b], uses["p", s, b] + 1)
                        kcs = [1] if blk == 0 else [0, 1]
                        for j in range(GRP):
                            for kc in kcs:
                                cols = bass.ds(g_v * HD, HD)
                                last = three(pv[:, HD * j:HD * (j + 1)],
                                             (wTb_hi[:, kc, P * j:P * (j + 1)], wTb_lo[:, kc, P * j:P * (j + 1)]),
                                             (vb_hi[:, blk - 1 + kc, cols], vb_lo[:, blk - 1 + kc, cols]),
                                             kc == kcs[0], kc == 1)
                        last.then_inc(pvb_ready, 1)
                    if s >= 3 or lag:
                        pe.wait_ge(pvb_free, t - 2)
                        if not isinstance(g, int) or t > 3:
                            pe.wait_ge(ot_free, t - 3)
                        for a in range(2):
                            last = nc.tensor.transpose(
                                score[1][:, HALF + P * a:HALF + P * (a + 1)],
                                osb[(s - 3) % 2][:, 2 * a:2 * a + 2, :].rearrange("p a d -> p (a d)"), ident[:, :])
                        last.then_inc(ot_ready, 1)
                    if ("k", 0) in uses and s == 0:
                        pe.wait_ge(kn_ready, g * 2 + 2)
                        for b in range(2):
                            before = uses["k", b]
                            if not isinstance(before, int) or before > 0:
                                pe.wait_ge(bm_free[b], before)
                            for i in range(4):
                                last = nc.tensor.transpose(
                                    trb[b][:, P * i:P * (i + 1)],
                                    kn[:, 4 * b + i, :, :].rearrange("p a d -> p (a d)"), ident[:, :])
                            last.then_inc(bm_ready[b], 1)

            steps(0, False, True, range(NB))
            with pe.Fori(1, KVH) as g:
                steps(g, True, True, range(NB))
            steps(KVH, True, False, range(3))
            segment(1)


_INS = ["x", "attn_norm_g", "mlp_norm_g", "a_w_qkv", "a_q_norm_g", "a_k_norm_g", "a_lambda_q1", "a_lambda_k1",
        "a_lambda_q2", "a_lambda_k2", "a_subln_g", "a_w_o", "kv_norm_g", "w_kv", "kv_k_norm_g", "b_w_q",
        "b_q_norm_g", "b_sinks", "b_w_o", "mlp_w_up", "mlp_w_down"]


def kernel(**inputs):
    import numpy as _np
    import concourse.bacc as _bacc
    from concourse import mybir as _mybir
    from concourse.bass_utils import run_bass_kernel_spmd as _run

    nc = _bacc.Bacc("TRN2", target_bir_lowering=False, num_devices=1)
    arrays, io = {}, {}
    for name in _INS:
        a = _np.ascontiguousarray(inputs[name])
        arrays[f"in_{name}"] = a
        io[name] = nc.dram_tensor(f"in_{name}", a.shape, _mybir.dt.from_np(a.dtype), kind="ExternalInput").ap()
    io["out"] = nc.dram_tensor("out", (1, S, D), F32, kind="ExternalOutput").ap()
    trunk(nc, io)
    r = _run(nc, [arrays], core_ids=[0])
    return r.results[0]["out"]
```

```python
from contextlib import ExitStack

import concourse.bass as bass
import numpy as np
from concourse import mybir

ALU = mybir.AluOpType
ACT = mybir.ActivationFunctionType
F32 = mybir.dt.float32
F32R = mybir.dt.float32r
I32 = mybir.dt.int32
AX_X = mybir.AxisListType.X

P = 128
D = 1024
S = 1024
KC = D // P
NB = S // P
HALF = 512
NH = 8
HD = 64
KVH = 4
GRP = 4
CH = 64
FF = 4096
EPS = 1e-6
LAM0 = 0.2
QUARTERS = 4
SEG = KC + QUARTERS * 2 * KC
MASK = -1e30
LOWEST = -3.0e38
O_STEP = 4
CONSTS = 18


def lag_banks(s):
    return s // 4 + 1


def plan_a(first_use, attn, tail, qkv):
    uses = {}
    n = first_use
    for s in range(NB):
        if (s == 0 and tail) or (s > 0 and attn):
            for i in range(lag_banks((s - 1) % NB)):
                uses["lag", s, i] = n
                n += 1
        if s % 2 == 1 and (attn if s == 1 else qkv):
            uses["pair", s] = n
            n += 1
        if s == O_STEP and tail:
            for i in range(2):
                uses["o", i] = n
                n += 1
    return uses, n


def plan_b(first0, first1, steps, has_lag):
    uses = {}
    n = [first0, first1]
    for s in steps:
        if (s >= 2 or has_lag) and (len(steps) == NB or s < 2):
            for b in range(2):
                if b == 1 or s != 2:
                    uses["p", s, b] = n[b]
                    n[b] += 1
        if s == 0 and len(steps) == NB:
            for b in range(2):
                uses["k", b] = n[b]
                n[b] += 1
    return uses, n


def trunk(nc, io):
    ctx = ExitStack()
    with ctx:
        def sb(name, shape, dt=F32, scope=ctx):
            return scope.enter_context(nc.sbuf_tensor(name, shape, dt))

        def sem(name):
            return ctx.enter_context(nc.semaphore(name))

        ident = sb("ident", [P, P])
        ones = sb("ones", [P, P])
        gains = sb("gains", [P, 5, KC])
        heads64 = sb("heads64", [P, 8])
        gsub = sb("gsub", [P, 1])
        lam_in = sb("lam_in", [HD, 4])
        lam_pr = sb("lam_pr", [HD, 2])
        lam_e = sb("lam_e", [P, 2])
        neg_lam = sb("neg_lam", [P, 1])
        sink_col = sb("sink_col", [16, 1])
        sink_dg = sb("sink_dg", [16, 16])
        sinks = sb("sinks", [P, 16])
        slopes = sb("slopes", [P, NH + 16])
        k_gain = sb("k_gain", [P, NH])
        msq = sb("msq", [P, NB])
        row_r = sb("row_r", [P, NB])
        chain_v = sb("chain_v", [P, 8])
        chain_s = sb("chain_s", [P, NB * KVH], I32)
        chain_t = sb("chain_t", [P, 2, NB])
        chain_p = sb("chain_p", [P, 2, NB * KVH])
        chain_o = sb("chain_o", [P, NB])
        chain_q = [sb(f"chain_q{i}", [P, 8]) for i in range(2)]
        stat_m = sb("stat_m", [P, 8])
        xT = sb("xT", [P, KC, S])

        scope_d = ExitStack()
        a_hi = sb("a_hi", [P, KC, S], F32R, scope_d)
        a_lo = sb("a_lo", [P, KC, S], F32R, scope_d)
        scope_d2 = ExitStack()
        b_hi = sb("b_hi", [P, KC, S], F32R, scope_d2)
        b_lo = sb("b_lo", [P, KC, S], F32R, scope_d2)
        scope_w = ExitStack()
        w_raw = [sb(f"w_raw{i}", [P, KC, P], F32, scope_w) for i in range(2)]
        w_hi = [sb(f"w_hi{i}", [P, KC, P], F32R, scope_w) for i in range(2)]
        w_lo = [sb(f"w_lo{i}", [P, KC, P], F32R, scope_w) for i in range(2)]
        e1 = [sb(f"e1_{i}", [P, HALF], F32, scope_w) for i in range(2)]
        e2 = [sb(f"e2_{i}", [P, HALF], F32, scope_w) for i in range(2)]
        ss = sb("ss", [P, S], F32, scope_w)
        r2 = sb("r2", [P, S], F32, scope_w)
        scope_w.close()
        scope_wb = ExitStack()
        wb_raw = sb("wb_raw", [P, KC, 256], F32, scope_wb)
        wb_hi = sb("wb_hi", [P, KC, 256], F32R, scope_wb)
        wb_lo = sb("wb_lo", [P, KC, 256], F32R, scope_wb)
        dist_b = sb("dist_b", [P, 256], F32, scope_wb)
        bias_b = sb("bias_b", [P, GRP, 256], F32, scope_wb)
        osum = sb("osum", [P, GRP, HD], F32, scope_wb)
        osb = [sb(f"osb{i}", [P, GRP, HD], F32, scope_wb) for i in range(2)]
        qraw_b = [sb(f"qraw_b{i}", [P, 256], F32, scope_wb) for i in range(4)]
        sq_b = sb("sq_b", [P, 256], F32, scope_wb)
        stat_k = sb("stat_k", [P, NB * KVH], F32, scope_wb)
        chain_k = sb("chain_k", [P, NB * KVH], F32, scope_wb)
        chain_b = [sb(f"chain_b{i}", [P, GRP], F32, scope_wb) for i in range(4)]
        rstd_k = sb("rstd_k", [P, NB, KVH], F32, scope_wb)
        rstd_q = [sb(f"rstd_q{i}", [P, GRP], F32, scope_wb) for i in range(4)]
        mx_b = sb("mx_b", [P, GRP], F32, scope_wb)
        nm_b = [sb(f"nm_b{i}", [P, GRP], F32, scope_wb) for i in range(2)]
        esin_b = [sb(f"esin_b{i}", [P, GRP], F32, scope_wb) for i in range(2)]
        es_b = [sb(f"es_b{i}", [P, GRP], F32, scope_wb) for i in range(2)]
        sm_b = [sb(f"sm_b{i}", [P, GRP], F32, scope_wb) for i in range(2)]
        den_b = sb("den_b", [P, GRP], F32, scope_wb)
        rc_b = sb("rc_b", [P, GRP], F32, scope_wb)
        scope_wb.close()
        scope_d2.close()
        scope_a = ExitStack()
        v_hi = [sb(f"v_hi{i}", [P, NB, P], F32R, scope_a) for i in range(2)]
        v_lo = [sb(f"v_lo{i}", [P, NB, P], F32R, scope_a) for i in range(2)]
        kT_hi = [sb(f"kT_hi{i}", [P, S], F32R, scope_a) for i in range(2)]
        kT_lo = [sb(f"kT_lo{i}", [P, S], F32R, scope_a) for i in range(2)]
        qT_hi = sb("qT_hi", [P, S], F32R, scope_a)
        qT_lo = sb("qT_lo", [P, S], F32R, scope_a)
        p0 = [sb(f"p0_{i}", [P, S], F32, scope_a) for i in range(2)]
        dist_a = sb("dist_a", [P, S], F32, scope_a)
        p1 = sb("p1", [P, S], F32, scope_a)
        wT_hi = sb("wT_hi", [P, NB, P], F32R, scope_a)
        wT_lo = sb("wT_lo", [P, NB, P], F32R, scope_a)
        wa_raw = [sb(f"wa_raw{i}", [P, 2, 3, P], F32, scope_a) for i in range(4)]
        wa_hi = sb("wa_hi", [P, KC, 3 * P], F32R, scope_a)
        wa_lo = sb("wa_lo", [P, KC, 3 * P], F32R, scope_a)
        qk2 = sb("qk2", [P, 4, 2 * P], F32, scope_a)
        sq_a = sb("sq_a", [P, 2 * P], F32, scope_a)
        oraw = sb("oraw", [P, NB, P], F32, scope_a)
        rstd_qk = [sb(f"rstd_qk{i}", [P, 8], F32, scope_a) for i in range(2)]
        rstd_o = sb("rstd_o", [P, NB], F32, scope_a)
        oss = sb("oss", [P, NB], F32, scope_a)
        ssum = [sb(f"ssum{i}", [P, 2, NB], F32, scope_a) for i in range(2)]
        s0sq = sb("s0sq", [P, NB], F32, scope_a)
        mx_a = sb("mx_a", [P, 2], F32, scope_a)
        nm_a = sb("nm_a", [P, 2], F32, scope_a)
        rcp_a = sb("rcp_a", [P, 1], F32, scope_a)
        coef_a = sb("coef_a", [P, 1], F32, scope_a)
        scope_a.close()
        scope_x = ExitStack()
        x_tok = sb("x_tok", [P, NB, D], F32, scope_x)
        x_stage = [sb(f"x_stage{i}", [P, HALF], F32, scope_x) for i in range(4)]
        x_junk = sb("x_junk", [P, D], F32, scope_x)
        scope_x.close()
        scope_d.close()
        scope_b = ExitStack()
        kraw = sb("kraw", [P, NB, 256], F32, scope_b)
        vb = sb("vb", [P, NB, KVH, 2, HD], F32R, scope_b)
        kn = sb("kn", [P, NB, 2, HD], F32, scope_b)
        kTb_hi = sb("kTb_hi", [P, S], F32R, scope_b)
        kTb_lo = sb("kTb_lo", [P, S], F32R, scope_b)
        pb = [sb(f"pb{i}", [P, GRP, 256], F32, scope_b) for i in range(2)]
        wTb_hi = sb("wTb_hi", [P, 2, HALF], F32R, scope_b)
        wTb_lo = sb("wTb_lo", [P, 2, HALF], F32R, scope_b)
        qTb_hi = [sb(f"qTb_hi{i}", [P, 2, P], F32R, scope_b) for i in range(2)]
        qTb_lo = [sb(f"qTb_lo{i}", [P, 2, P], F32R, scope_b) for i in range(2)]
        scope_b.close()
        oT = xT

        score = [ctx.enter_context(nc.psum_tensor(f"score{i}", [P, 2 * HALF], F32)) for i in range(2)]
        proj = ctx.enter_context(nc.psum_tensor("proj", [P, HALF], F32))
        trb = [ctx.enter_context(nc.psum_tensor(f"trb{i}", [P, HALF], F32)) for i in range(2)]
        pv = ctx.enter_context(nc.psum_tensor("pv", [P, HALF], F32))
        bank = [[score[i][:, HALF * h:HALF * (h + 1)] for h in range(2)] for i in range(2)]

        x_dram = nc.dram_tensor("xT_dram", [P, KC, S], F32, kind="Internal").ap()

        const_in, made, made2, made3 = sem("const_in"), sem("made"), sem("made2"), sem("made3")
        small_mm, sinks_done, lam_exp = sem("small_mm"), sem("sinks_done"), sem("lam_exp")
        x_half_in = [sem(f"x_half_in{i}") for i in range(2)]
        x_tr, x_hi_done, x_staged, x_bank_free = sem("x_tr"), sem("x_hi_done"), sem("x_staged"), sem("x_bank_free")
        x_stored = [sem(f"x_stored{i}") for i in range(4)]
        row_stats, gain_in = sem("row_stats"), sem("gain_in")
        wa_in = [sem(f"wa_in{i}") for i in range(4)]
        wa_hi_done, wa_lo_done = sem("wa_hi_done"), sem("wa_lo_done")
        qkv_ready, qkv_free, qkv_copied, sq_done, red_done = (
            sem("qkv_ready"), sem("qkv_free"), sem("qkv_copied"), sem("sq_done"), sem("red_done"))
        qk_rstd, qk_normed, pair_hi, kT_done = sem("qk_rstd"), sem("qk_normed"), sem("pair_hi"), sem("kT_done")
        scores_ready, score_max, nm_ready, exp_done, mixed = (
            sem("scores_ready"), sem("score_max"), sem("nm_ready"), sem("exp_done"), sem("mixed"))
        tr_ready, tr_free = sem("tr_ready"), [sem(f"tr_free{i}") for i in range(2)]
        wT_hi_done, pv_ready, pv_free = sem("wT_hi_done"), sem("pv_ready"), sem("pv_free")
        o_rstd, o_normed = sem("o_rstd"), sem("o_normed")
        o_split_hi, o_split, x_back = sem("o_split_hi"), sem("o_split"), sem("x_back")
        w_in = [sem(f"w_in{i}") for i in range(2)]
        w_hi_done, w_lo_done, panel_half = sem("w_hi_done"), sem("w_lo_done"), sem("panel_half")
        bank_free = [[sem(f"bank_free{i}{h}") for h in range(2)] for i in range(2)]
        u_hi_done, u_sq_done, u_split = sem("u_hi_done"), sem("u_sq_done"), sem("u_split")
        x_added, b_hi_done, b_split, x_sq, ss_added = (
            sem("x_added"), sem("b_hi_done"), sem("b_split"), sem("x_sq"), sem("ss_added"))
        ss_sum, r2_ready, x_parked = sem("ss_sum"), sem("r2_ready"), sem("x_parked")
        wb_in, wb_hi_done, wb_lo_done = sem("wb_in"), sem("wb_hi_done"), sem("wb_lo_done")
        pb_ready, pb_free, sqb_done, redb_done = sem("pb_ready"), sem("pb_free"), sem("sqb_done"), sem("redb_done")
        vb_hi_done, rstdb, qb_normed, kn_ready = sem("vb_hi_done"), sem("rstdb"), sem("qb_normed"), sem("kn_ready")
        bm_ready, bm_free = [sem(f"bm_ready{i}") for i in range(2)], [sem(f"bm_free{i}") for i in range(2)]
        bm_hi = [sem(f"bm_hi{i}") for i in range(2)]
        qt_ready, qt_hi, qt_free = sem("qt_ready"), sem("qt_hi"), sem("qt_free")
        sb_ready, sb_max, nmb_ready, expb_done = sem("sb_ready"), sem("sb_max"), sem("nmb_ready"), sem("expb_done")
        pvb_ready, pvb_free, ot_ready, ot_free = sem("pvb_ready"), sem("pvb_free"), sem("ot_ready"), sem("ot_free")
        biasb_ready, pz, osb_ready = sem("biasb_ready"), sem("pz"), sem("osb_ready")
        out_tr, out_staged = sem("out_tr"), sem("out_staged")
        dve_passed, act_passed = sem("dve_passed"), sem("act_passed")
        out_done = [sem(f"out_done{i}") for i in range(2)]

        block = ctx.enter_context(nc.Block())

        def walk(eng, seg, run, before_down=None):
            first = seg * SEG

            def pairs(kind, half_start, quarter, lo, hi, **flags):
                def body(j):
                    for i in range(2):
                        run(kind, (half_start + j) * 2 + i, half_start + j, j * 2 + i, quarter, i, **flags)
                if hi - lo == 1:
                    body(lo)
                else:
                    with eng.Fori(lo, hi) as j:
                        body(j)

            def quarter_of(q, **flags):
                up = q * KC + (first + KC) // 2
                down = up + KC // 2
                n = KC // 2
                if flags.get("first"):
                    pairs("up", up, q, 0, 1, head=True, **flags)
                    pairs("up", up, q, 1, n, **flags)
                    if before_down:
                        before_down()
                    pairs("down", down, q, 0, 1, head=True, **flags)
                    pairs("down", down, q, 1, n, **flags)
                    return
                pairs("up", up, q, 0, n, **flags)
                if not flags.get("last"):
                    pairs("down", down, q, 0, n, **flags)
                    return
                pairs("down", down, q, 0, 1, head=True, **flags)
                pairs("down", down, q, 1, n - 1, **flags)
                pairs("down", down, q, n - 1, n, tail=True, **flags)

            pairs("wo", first // 2, 0, 0, KC // 2)
            quarter_of(0, first=True)
            with eng.Fori(1, QUARTERS - 1) as q:
                quarter_of(q)
            quarter_of(QUARTERS - 1, last=True)

        def chunk_of(t, c, half):
            cols = slice(HALF * half, HALF * (half + 1))
            if isinstance(c, int):
                return t[:, c, cols]
            return t[:, bass.ds(c, 1), cols].rearrange("p a n -> p (a n)")

        def one(t, c):
            return t[:, c:c + 1] if isinstance(c, int) else t[:, bass.ds(c, 1)]

        def run_heads(eng, head):
            head(-1, 1, False, False, True, True)
            head(0, 0, True, False, True, True)
            with eng.Fori(0, 2) as i:
                head(2 * i + 1, 1, True, True, True, True)
                head(2 * i + 2, 0, True, True, True, True)
            head(NH - 3, 1, True, True, True, True)
            head(NH - 2, 0, True, True, True, False)
            head(NH - 1, 1, True, True, False, False)

        def uses_a(h, attn, tail, qkv):
            if isinstance(h, int) and h == -1:
                k = 18
            elif isinstance(h, int) and h == 0:
                k = 3
            else:
                k = -1
            plan, _ = plan_a(k, attn, tail, qkv)
            return {key: (n % 2, h * 9 + n // 2, h * 18 + n) for key, n in plan.items()}

        def up_half(seg, quarter, chunk, half):
            return seg * 64 + quarter * 16 + chunk * 2 + half

        def out_index(chunk, half):
            return chunk * 2 + half

        def rsqrt_guess(dve, out, vec, n):
            v, sh = vec[:, 0:n], chain_s[:, 0:n]
            dve.drain()
            dve.tensor_scalar(sh, v.bitcast(I32), 1, None, ALU.logical_shift_right)
            dve.drain()
            return dve.tensor_scalar(out.bitcast(I32), sh, -1.0, float(0x5F3759DF), ALU.mult, ALU.add)

        def rsqrt_steps(eng, out, vec, t, n):
            v, t, half_v = vec[:, 0:n], t[:, 0, 0:n], t[:, 1, 0:n]
            for i in range(3):
                if i:
                    eng.drain()
                eng.tensor_tensor(t, out, out, ALU.mult)
                if i == 0:
                    eng.tensor_scalar(half_v, v, -0.5, None, ALU.mult)
                eng.drain()
                eng.tensor_tensor(t, t, half_v, ALU.mult)
                eng.drain()
                eng.tensor_scalar(t, t, 1.5, None, ALU.add)
                eng.drain()
                last = eng.tensor_tensor(out, out, t, ALU.mult)
            return last

        def pair_of(s, par):
            if s == 1:
                return par, slice(6 * P, 8 * P)
            return 1 - par, slice((s - 3) * P, (s - 1) * P)

        def proj_bank(n):
            return pv if isinstance(n, int) and n < 2 * NB and n % 2 == 0 else proj

        def qkv_bank(h, s):
            return pv if isinstance(h, int) and h < 0 and s % 2 == 0 else proj

        def score_cols(j, lo):
            first = HALF * (j % 2) + 256 * (j // 2)
            return score[0][:, first + lo:first + 256]

        def uses_b(g, lag, proj_on, which):
            if isinstance(g, int) and g == 0:
                plan, _ = plan_b(0, 0, list(which), False)
                return plan
            plan, _ = plan_b(-2, -2, list(which), True)
            return {k: (g * (8 if k[-1] == 0 else 9)) + n for k, n in plan.items()}

        last_uses = {("lag", 0, i): ((140 + i) % 2, (140 + i) // 2, 140 + i) for i in range(2)}
        last_uses.update({("o", i): ((142 + i) % 2, (142 + i) // 2, 142 + i) for i in range(2)})

        @block.sync
        def _(sp):
            def col(dst, src, done):
                sp.dma_start(dst, src, allow_slow_non_contiguous=True).then_inc(done, 16)

            col(gains[:, 0, :], io["attn_norm_g"][0].rearrange("(c p) -> p c", p=P), gain_in)
            for b in range(NB):
                sp.dma_start(x_tok[:, b, :], io["x"][0, P * b:P * (b + 1), :]).then_inc(x_half_in[b // 4], 16)
            small = [(gains[:, i + 1, :], src.rearrange("(c p) -> p c", p=P))
                     for i, src in enumerate((io["mlp_norm_g"][0], io["mlp_norm_g"][1],
                                              io["kv_norm_g"], io["attn_norm_g"][1]))]
            for i, src in enumerate((io["a_q_norm_g"][0], io["a_k_norm_g"][0], io["b_q_norm_g"][0], io["kv_k_norm_g"])):
                for half in range(2):
                    small.append((heads64[HD * half:HD * (half + 1), i:i + 1], src.rearrange("(p a) -> p a", a=1)))
            small.append((gsub[:, :], io["a_subln_g"][0].rearrange("(p a) -> p a", a=1)))
            for i, name in enumerate(("a_lambda_q1", "a_lambda_k1", "a_lambda_q2", "a_lambda_k2")):
                small.append((lam_in[:, i:i + 1], io[name][0].rearrange("(p a) -> p a", a=1)))
            small.append((sink_col[:, :], io["b_sinks"][0].rearrange("(p a) -> p a", a=1)))
            assert len(small) == CONSTS

            wqkv = io["a_w_qkv"][0].rearrange("(k p) (t n) -> p k t n", p=P, t=3)

            def load_wa(hq, i):
                for t in range(3):
                    sp.dma_start(wa_raw[i][:, :, t, :],
                                 wqkv[:, 2 * i:2 * i + 2, t, bass.ds(hq * P, P)]).then_inc(wa_in[i], 16)

            for i in range(4):
                load_wa(0, i)
            for n in range(2 * KC):
                sp.wait_ge(x_staged, n + 1)
                sp.dma_start(x_dram[:, n % KC, HALF * (n // KC):HALF * (n // KC + 1)],
                             x_stage[n % 4][:, :]).then_inc(x_stored[n % 4], 16)
                col(*small.pop(0), const_in)
            for dst, src in small:
                col(dst, src, const_in)
            with sp.Fori(1, NH) as hq:
                for i in range(4):
                    sp.wait_ge(wa_lo_done, hq * 4 + (i - 3))
                    load_wa(hq, i)

            w_of = {
                "wo": (io["a_w_o"][0], io["b_w_o"][0]),
                "up": (io["mlp_w_up"][0], io["mlp_w_up"][1]),
                "down": (io["mlp_w_down"][0], io["mlp_w_down"][1]),
            }

            def segment(seg):
                def load(kind, panel, chunk, quarter, slot):
                    w = w_of[kind][seg].rearrange("(k p) n -> p k n", p=P)
                    if kind == "up":
                        src = w[:, :, bass.ds((quarter * KC + chunk) * P, P)]
                    elif kind == "wo":
                        src = w[:, :, bass.ds(chunk * P, P)]
                    else:
                        src = w[:, bass.ds(quarter * KC, KC), bass.ds(chunk * P, P)]
                    if not isinstance(panel, int) or panel >= 2:
                        sp.wait_ge(w_lo_done, panel - 1)
                    sp.dma_start(w_raw[slot][:, :, :], src).then_inc(w_in[slot], 16)

                if seg == 0:
                    sp.wait_ge(qkv_ready, NH * NB)
                    for i in range(4):
                        sp.wait_ge(x_stored[i], 4 * 16)
                else:
                    sp.wait_ge(ot_free, 32)
                    sp.wait_ge(x_parked, 16 * 2 * KC)
                first = seg * SEG
                for i in range(2):
                    load("wo", first + i, i, 0, i)
                for c in range(KC):
                    sp.wait_ge(o_split, seg * KC + c + 1)
                    sp.dma_start(xT[:, c, :], x_dram[:, c, :]).then_inc(x_back, 16)
                with sp.Fori(1, KC // 2) as j:
                    for i in range(2):
                        load("wo", j * 2 + (first + i), j * 2 + i, 0, i)
                with sp.Fori(0, QUARTERS) as q:
                    for kind, start in (("up", first + KC), ("down", first + 2 * KC)):
                        with sp.Fori(0, KC // 2) as j:
                            for i in range(2):
                                load(kind, q * (2 * KC) + j * 2 + (start + i), j * 2 + i, q, i)

            segment(0)
            sp.wait_ge(panel_half, 2 * SEG)
            wkv = io["w_kv"].rearrange("(k p) n -> p k n", p=P)
            wq = io["b_w_q"][0].rearrange("(k p) n -> p k n", p=P)
            for j in range(2):
                if j:
                    sp.wait_ge(wb_lo_done, KC * j)
                sp.dma_start(wb_raw[:, :, :], wkv[:, :, 256 * j:256 * (j + 1)]).then_inc(wb_in, 16)
            with sp.Fori(0, KVH) as g:
                sp.wait_ge(wb_lo_done, g * KC + 2 * KC)
                sp.dma_start(wb_raw[:, :, :], wq[:, :, bass.ds(g * 256, 256)]).then_inc(wb_in, 16)
            segment(1)

        @block.gpsimd
        def _(pool):
            pool.memset(ident[:, :], 0.0).then_inc(made, 1)
            pool.memset(ones[:, :], 1.0).then_inc(made, 1)
            for h in range(NH):
                pool.memset(slopes[:, h:h + 1], float(np.float32(2.0 ** (-8.0 * (h + 1) / NH))))
                pool.memset(k_gain[:, h:h + 1], float(np.float32(2.0 ** (8.0 * (h + 1) / NH))))
            for h in range(16):
                pool.memset(slopes[:, NH + h:NH + h + 1], float(np.float32(2.0 ** (-8.0 * (h + 1) / 16))))
            pool.wait_ge(made, 2)
            pool.affine_select(out=ident[:, :], in_=ident[:, :], compare_op=ALU.not_equal, fill=1.0, base=0,
                               pattern=[[-1, P]], channel_multiplier=1).then_inc(made2, 1)

            def neg_distance(dist, junk, n, base, masks):
                for t, sign in ((dist, 1), (junk, -1)):
                    pool.iota(t, [[-sign, n]], base=sign * base, channel_multiplier=sign,
                              allow_small_or_imprecise_dtypes=True)
                    pool.drain()
                    pool.affine_select(out=t, in_=t, compare_op=ALU.is_ge, fill=0.0, base=-sign * base,
                                       pattern=[[sign, n]], channel_multiplier=-sign)
                pool.drain()
                pool.tensor_tensor(dist, dist, junk, ALU.add)
                for rows, cols in masks:
                    pool.drain()
                    last = pool.memset(dist[rows, cols], MASK)
                return last

            neg_distance(dist_a[:, :], p0[1][:, :], S, S - P, [(slice(0, CH), slice(S - CH, S))]).then_inc(made3, 1)

            def norm_steps(out, vec, n):
                rsqrt_steps(pool, out, vec, chain_p, n)
                pool.drain()

            def head(h, par, attn, tail, qkv, more):
                for s in range(NB):
                    if s % 2 == 1 and qkv:
                        pool.wait_ge(qk_rstd, h * 4 + 4 + s // 2 + 1)
                        norm_steps(rstd_qk[s // 2 % 2][:, :], chain_q[s // 2 % 2], 8)
                        v = qk2[:, s % 4 - 1:s % 4 + 1, :].rearrange("p a (b d) -> p (a b) d", d=HD)
                        pool.tensor_tensor(v, v, rstd_qk[s // 2 % 2][:, :].unsqueeze(2).to_broadcast([P, 8, HD]), ALU.mult)\
                            .then_inc(qk_normed, 1)
                    if s == 1 and tail:
                        pool.wait_ge(o_rstd, h)
                        norm_steps(rstd_o[:, :], chain_o, NB)
                        pool.tensor_tensor(oraw[:, :, :], oraw[:, :, :],
                                           rstd_o[:, :].unsqueeze(2).to_broadcast([P, NB, P]), ALU.mult)\
                            .then_inc(o_normed, 1)

            run_heads(pool, head)
            pool.wait_ge(o_rstd, NH)
            norm_steps(rstd_o[:, :], chain_o, NB)
            pool.tensor_tensor(oraw[:, :, :], oraw[:, :, :],
                               rstd_o[:, :].unsqueeze(2).to_broadcast([P, NB, P]), ALU.mult).then_inc(o_normed, 1)

            def add_square(z, half, clears):
                pool.wait_ge(x_sq, z + 1)
                pool.wait_ge(ss_added, z + (clears - 1))
                sh = ss[:, HALF * half:HALF * (half + 1)]
                pool.tensor_tensor(sh, sh, e1[half][:, :], ALU.add).then_inc(ss_added, 1)

            def segment(seg):
                def run(kind, panel, use, chunk, quarter, slot, **flags):
                    for half in range(2):
                        if kind == "wo":
                            add_square(chunk * 2 + (32 * seg + half), half, 2 + 4 * seg)
                        elif kind == "up":
                            u = up_half(seg, quarter, chunk, half)
                            pool.wait_ge(bank_free[slot][half], use + 1)
                            if not isinstance(u, int) or u >= 2:
                                pool.wait_ge(u_split, u - 1)
                            if not isinstance(quarter, int) or quarter or seg:
                                pool.wait_ge(x_added, up_half(seg, quarter, 0, half) - 1)
                            pool.tensor_tensor(e2[half][:, :], e1[half][:, :], e1[half][:, :], ALU.mult)\
                                .then_inc(u_sq_done, 1)
                        else:
                            v = up_half(seg, quarter, chunk, half)
                            pool.wait_ge(bank_free[slot][half], use + 1)
                            x_c = chunk_of(xT, chunk, half)
                            if flags.get("last") and seg == 1:
                                if not flags.get("head") or slot:
                                    pool.wait_ge(out_tr, out_index(chunk, half) - 1)
                                pool.tensor_tensor(e1[half][:, :], x_c, e2[half][:, :], ALU.add).then_inc(x_added, 1)
                                continue
                            pool.tensor_tensor(x_c, x_c, e2[half][:, :], ALU.add).then_inc(x_added, 1)
                    if kind == "down" and flags.get("last") and seg == 0:
                        for half in range(2):
                            add_square(chunk * 2 + (16 + half), half, 4)

                def clear():
                    for half in range(2):
                        pool.memset(ss[:, HALF * half:HALF * (half + 1)], 0.0).then_inc(ss_added, 1)

                if seg == 0:
                    pool.wait_ge(tr_ready, 144)
                    clear()
                    walk(pool, seg, run, before_down=lambda: (pool.wait_ge(ss_sum, 2), clear()))
                else:
                    pool.wait_ge(ot_free, 32)
                    clear()
                    walk(pool, seg, run)

            segment(0)

            pool.wait_ge(panel_half, 2 * SEG)
            pool.wait_ge(ss_sum, 3)
            pool.wait_ge(u_split, 64)
            neg_distance(dist_b[:, :], pb[0][:, 0, :], 256, P,
                         [(slice(0, CH), slice(256 - CH, 256)), (slice(CH, P), slice(0, P))])
            pool.drain()
            for i in range(2):
                pool.memset(pb[i][:, :, :], 0.0).then_inc(pz, 1)

            def q_norm(t, par):
                pool.wait_ge(rstdb, t + 2)
                pool.wait_ge(pb_free, t + 2 * NB + 1)
                norm_steps(rstd_q[par][:, :], chain_b[par], GRP)
                v = qraw_b[par][:, :].rearrange("p (a d) -> p a d", d=HD)
                pool.tensor_tensor(v, v, rstd_q[par][:, :].unsqueeze(2).to_broadcast([P, GRP, HD]), ALU.mult)\
                    .then_inc(qb_normed, 1)

            def group(g, lag):
                if lag:
                    pool.wait_ge(sb_max, g * NB - (NB - 1))
                else:
                    pool.wait_ge(rstdb, 1)
                    pool.wait_ge(pb_free, NB)
                    norm_steps(rstd_k[:, :, :].rearrange("p a b -> p (a b)"), chain_k, NB * KVH)
                for d in range(2):
                    pool.tensor_tensor(kn[:, :, d, :], kraw[:, :, bass.ds(g * HD, HD)],
                                       rstd_k[:, :, bass.ds(g, 1)].to_broadcast([P, NB, HD]), ALU.mult)\
                        .then_inc(kn_ready, 1)
                for s in range(NB):
                    if s == 1:
                        if lag:
                            pool.wait_ge(sb_max, g * NB)
                        for j in range(GRP):
                            pool.tensor_tensor(bias_b[:, j, :], dist_b[:, :],
                                               one(slopes, g * GRP + (NH + j)).to_broadcast([P, 256]), ALU.mult)\
                                .then_inc(biasb_ready, 1)
                    q_norm(g * NB + s, s % 4)

            group(0, False)
            with pool.Fori(1, KVH) as g:
                group(g, True)
            segment(1)

        @block.scalar
        def _(act):
            def copy(out, in_, scale=1.0):
                return nc.scalar.activation(out, in_, ACT.Copy, scale=scale)

            act.wait_ge(gain_in, 16)
            for n in range(2 * KC):
                half, c = divmod(n, KC)
                act.wait_ge(x_tr, n + 1)
                ps = bank[n % 2][n // 2 % 2]
                copy(a_hi[:, c, HALF * half:HALF * (half + 1)], ps, gains[:, 0, c:c + 1]).then_inc(x_hi_done, 1)
                if n >= 4:
                    act.wait_ge(x_stored[n % 4], 16 * (n // 4))
                copy(x_stage[n % 4][:, :], ps).then_inc(x_staged, 1)

            def wa_split(hq):
                if not isinstance(hq, int) or hq > 0:
                    act.wait_ge(qkv_ready, hq * NB)
                for i in range(4):
                    act.wait_ge(wa_in[i], hq * 48 + 48)
                    copy(wa_hi[:, 2 * i:2 * i + 2, :].rearrange("p k n -> p (k n)"),
                         wa_raw[i][:, :, :, :].rearrange("p k t n -> p (k t n)")).then_inc(wa_hi_done, 1)

            def head(h, par, attn, tail, qkv, more):
                uses = uses_a(h, attn, tail, qkv)
                hq = h + 1
                for s in range(NB):
                    t = h * NB + s
                    lag = ("lag", s, 0) in uses
                    for i in range(2):
                        if ("lag", s, i) in uses:
                            b, _, n = uses["lag", s, i]
                            blocks = (s - 1) % NB + 1
                            cols = P * (min(4 * i + 4, blocks) - 4 * i)
                            act.wait_ge(tr_ready, n + 1)
                            copy(wT_hi[:, 4 * i:4 * i + cols // P, :].rearrange("p a n -> p (a n)"),
                                 trb[b][:, 0:cols]).then_inc(wT_hi_done, 1)
                    if attn:
                        keys = P * (s + 1)
                        act.wait_ge(nm_ready, t + 1)
                        act.sem_inc(act_passed, 1)
                        for c, p in ((0, p0[s % 2]), (1, p1)):
                            nc.scalar.activation(p[:, 0:keys], p[:, 0:keys], ACT.Exp, bias=nm_a[:, c:c + 1],
                                                 scale=one(slopes, h),
                                                 accum_out=ssum[par][:, c, s:s + 1]).then_inc(exp_done, 1)
                    if qkv:
                        act.wait_ge(qkv_ready, t + NB + 1)
                        if s == 0 and tail:
                            act.wait_ge(pv_ready, h * NB)
                        rows = qkv_bank(h, s)
                        copy(v_hi[1 - par][:, s, :], rows[:, 256:384], row_r[:, s:s + 1])
                        copy(qk2[:, s % 4, :], rows[:, 0:256]).then_inc(qkv_copied, 1)
                        if not isinstance(h, int) or h >= 0 or s:
                            act.wait_ge(red_done, t + NB)
                        act.wait_ge(qkv_copied, t + NB + 1)
                        nc.scalar.activation(sq_a[:, :], qk2[:, s % 4, :], ACT.Square).then_inc(sq_done, 1)
                    if ("pair", s) in uses:
                        b, _, n = uses["pair", s]
                        kp, cols = pair_of(s, par)
                        act.wait_ge(tr_ready, n + 1)
                        copy(qT_hi[:, cols], trb[b][:, 0:256])
                        copy(kT_hi[kp][:, cols], trb[b][:, 256:512], one(k_gain, h if s == 1 else hq)).then_inc(pair_hi, 1)
                    if s == NB - 1 and more:
                        wa_split(h + 2)
                    if s == O_STEP and tail:
                        evac_o(uses, h - 1)
                    if lag and (s - 1) % 4 == 3:
                        evac_pv(t - 1, (s - 1) % NB)

            def evac_o(uses, h):
                for i in range(2):
                    b, _, n = uses["o", i]
                    act.wait_ge(tr_ready, n + 1)
                    copy(chunk_of(oT, h, i), trb[b][:, :], gsub[:, 0:1]).then_inc(tr_free[b], 1)

            def evac_pv(t, s):
                act.wait_ge(pv_ready, t + 1)
                copy(oraw[:, s - 3:s + 1, :].rearrange("p a n -> p (a n)"), pv[:, :])
                act.drain()
                for i in range(4):
                    last = nc.scalar.activation(pv[:, P * i:P * (i + 1)], pv[:, P * i:P * (i + 1)], ACT.Square,
                                                accum_out=oss[:, s - 3 + i:s - 2 + i])
                last.then_inc(pv_free, 1)

            wa_split(0)
            for i in range(4):
                act.wait_ge(x_stored[i], 4 * 16)
            act.wait_ge(small_mm, 1)
            nc.scalar.activation(lam_e[:, :], proj[:, 0:2], ACT.Exp).then_inc(lam_exp, 1)
            act.wait_ge(const_in, 16 * CONSTS)
            act.wait_ge(row_stats, 1)
            run_heads(act, head)
            for i in range(2):
                b, _, n = last_uses["lag", 0, i]
                act.wait_ge(tr_ready, n + 1)
                copy(wT_hi[:, 4 * i:4 * i + 4, :].rearrange("p a n -> p (a n)"), trb[b][:, :]).then_inc(wT_hi_done, 1)
            evac_pv(NH * NB - 1, NB - 1)
            evac_o(last_uses, NH - 1)

            def split_panel(panel, use, slot):
                act.wait_ge(w_in[slot], use * 16 + 16)
                if not isinstance(panel, int) or panel >= 2:
                    act.wait_ge(panel_half, panel * 2 - 2)
                copy(w_hi[slot][:, :, :].rearrange("p k n -> p (k n)"),
                     w_raw[slot][:, :, :].rearrange("p k n -> p (k n)")).then_inc(w_hi_done, 1)

            def next_input(z, clears, chunk, half, gain):
                copy(chunk_of(b_hi, chunk, half), chunk_of(xT, chunk, half),
                     1.0 if gain is None else one(gains[:, gain, :], chunk)).then_inc(b_hi_done, 1)
                act.wait_ge(ss_added, z + (clears - 1))
                act.sem_inc(act_passed, 1)
                nc.scalar.activation(e1[half][:, :], chunk_of(xT, chunk, half), ACT.Square).then_inc(x_sq, 1)

            def segment(seg):
                def run(kind, panel, use, chunk, quarter, slot, **flags):
                    if not (flags.get("tail") and slot == 1):
                        split_panel(panel + 1, use + slot, 1 - slot)
                    for half in range(2):
                        if kind == "wo":
                            act.wait_ge(bank_free[slot][half], use + 1)
                            next_input(chunk * 2 + (32 * seg + half), 2 + 4 * seg, chunk, half, 1 + seg)
                        elif kind == "up":
                            u = up_half(seg, quarter, chunk, half)
                            act.wait_ge(panel_half, panel * 2 + half + 1)
                            if flags.get("first") and flags.get("head") and slot == 0:
                                act.wait_ge(ss_added, 18 + 36 * seg)
                            else:
                                act.wait_ge(u_sq_done, u - 1)
                            nc.scalar.activation(e1[half][:, :], bank[slot][half], ACT.Relu)\
                                .then_inc(bank_free[slot][half], 1)
                            act.wait_ge(bank_free[slot][half], use + 1)
                            nc.scalar.activation(chunk_of(a_hi, chunk, half), e1[half][:, :], ACT.Square)\
                                .then_inc(u_hi_done, 1)
                        elif flags.get("last") and seg == 0:
                            act.wait_ge(x_added, up_half(seg, quarter, chunk, half) + 1)
                            next_input(chunk * 2 + (16 + half), 4, chunk, half, None)
                            act.dma_start(
                                x_dram[:, bass.ds(chunk, 1), HALF * half:HALF * (half + 1)].rearrange("p a n -> p (a n)"),
                                chunk_of(xT, chunk, half)).then_inc(x_parked, 16)
                    if kind == "down" and flags.get("last") and seg == 1:
                        if slot or not flags.get("head"):
                            store_out(chunk - 1)
                    if flags.get("tail") and slot == 1 and seg == 1:
                        store_out(chunk)

                def store_out(chunk):
                    for half in range(2):
                        n = out_index(chunk, half)
                        act.wait_ge(out_tr, n + 1)
                        if not isinstance(n, int) or n >= 2:
                            act.wait_ge(out_done[half], chunk * 16)
                        stage = ss[:, HALF * half:HALF * (half + 1)]
                        copy(stage, (proj, pv)[half][:, :]).then_inc(out_staged, 1)
                        act.wait_ge(out_staged, n + 1)
                        act.dma_start(
                            io["out"][0].rearrange("(h b p) d -> p h b d", h=2, p=P)[:, half, :, bass.ds(chunk * P, P)],
                            stage.rearrange("p (b d) -> p b d", d=P)).then_inc(out_done[half], 16)

                for c in range(KC):
                    if seg == 0:
                        act.wait_ge(tr_free[0], 72)
                        act.wait_ge(tr_free[1], 72)
                    else:
                        act.wait_ge(ot_free, 32)
                    copy(a_hi[:, c, :], oT[:, c, :]).then_inc(o_split_hi, 1)
                    if c == 0:
                        split_panel(seg * SEG, seg * SEG // 2, 0)
                walk(act, seg, run)
                if seg == 1:
                    for half in range(2):
                        act.wait_ge(out_done[half], 16 * KC)

            segment(0)

            def wb_split(job, gain):
                act.wait_ge(wb_in, job * 16 + 16)
                if not isinstance(job, int) or job > 0:
                    act.wait_ge(pb_ready, job * NB)
                for k in range(KC):
                    copy(wb_hi[:, k, :], wb_raw[:, k, :], gains[:, gain, k:k + 1]).then_inc(wb_hi_done, 1)

            def raw_and_squares(n, dst, red):
                act.wait_ge(pb_ready, n + 1)
                if not isinstance(red, int) or red > 0:
                    act.wait_ge(redb_done, red)
                rows = proj_bank(n)[:, 0:256]
                nc.scalar.activation(sq_b[:, :], rows, ACT.Square).then_inc(sqb_done, 1)
                copy(dst, rows).then_inc(pb_free, 1)

            act.wait_ge(panel_half, 2 * SEG)
            act.wait_ge(ss_sum, 3)
            wb_split(0, 3)
            for s in range(NB):
                raw_and_squares(s, kraw[:, s, :], s)
            wb_split(1, 3)
            for s in range(NB):
                act.wait_ge(pb_ready, NB + s + 1)
                copy(vb[:, s, :, 0, :], proj_bank(NB + s)[:, 0:256].rearrange("p (a d) -> p a d", d=HD),
                     row_r[:, s:s + 1]).then_inc(vb_hi_done, 1)

            def project_rows(t, s):
                raw_and_squares(t + 2 * NB, qraw_b[s % 4][:, :], t + NB)

            def steps(g, lag, proj_on, which, more=True):
                uses = uses_b(g, lag, proj_on, which)
                for s in which:
                    t = g * NB + s
                    if (s >= 1 or lag) and (proj_on or s == 0):
                        act.wait_ge(qt_ready, t)
                        copy(qTb_hi[(s - 1) % 2][:, :, :].rearrange("p a n -> p (a n)"), score[1][:, 0:256])\
                            .then_inc(qt_hi, 1)
                    for b in range(2):
                        if ("p", s, b) in uses:
                            act.wait_ge(bm_ready[b], uses["p", s, b] + 1)
                            copy(wTb_hi[:, b, :], trb[b][:, :]).then_inc(bm_hi[b], 1)
                    if proj_on and (s < NB - 1 or more):
                        project_rows(t + 1, s + 1)
                        if s == NB - 2 and more:
                            wb_split(g + 3, 4)
                    if (s >= 1 or lag) and (proj_on or s == 0):
                        par, lo = (s - 1) % 2, (P if s == 1 else CH)
                        act.wait_ge(nmb_ready, t)
                        for j in range(GRP):
                            nc.scalar.activation(pb[par][:, j, lo:256], pb[par][:, j, lo:256], ACT.Exp,
                                                 bias=nm_b[par][:, j:j + 1], accum_out=sm_b[par][:, j:j + 1])
                        nc.scalar.activation(es_b[par][:, :], esin_b[par][:, :], ACT.Exp).then_inc(expb_done, 1)
                    if s >= 3 or lag:
                        act.wait_ge(ot_ready, t - 2)
                        o_t = (s - 3) % NB
                        g_o = g if s >= 3 else g - 1
                        dst = oT[:, bass.ds(g_o * 2, 2), P * o_t:P * (o_t + 1)]
                        copy(dst, score[1][:, HALF:HALF + 256].rearrange("p (a n) -> p a n", a=2)).then_inc(ot_free, 1)
                    if ("k", 0) in uses and s == 0:
                        for b in range(2):
                            act.wait_ge(bm_ready[b], uses["k", b] + 1)
                            copy(kTb_hi[:, HALF * b:HALF * (b + 1)], trb[b][:, :], heads64[:, 5:6])\
                                .then_inc(bm_hi[b], 1)

            act.wait_ge(x_parked, 16 * 2 * KC)
            act.wait_ge(b_split, 32)
            act.wait_ge(pz, 2)
            wb_split(2, 4)
            project_rows(0, 0)
            steps(0, False, True, range(NB))
            with act.Fori(1, KVH - 1) as g:
                steps(g, True, True, range(NB))
            steps(KVH - 1, True, True, range(NB), more=False)
            steps(KVH, True, False, range(3))
            segment(1)

        @block.vector
        def _(dve):
            def low(out, full, hi, scale=None):
                if scale is None:
                    return nc.vector.tensor_tensor(out, full, hi.bitcast(F32), ALU.subtract)
                return nc.vector.scalar_tensor_tensor(out=out, in0=full, scalar=scale, in1=hi.bitcast(F32),
                                                      op0=ALU.mult, op1=ALU.subtract)

            dve.wait_ge(gain_in, 16)
            for n in range(2 * KC):
                half, c = divmod(n, KC)
                cols = slice(HALF * half, HALF * (half + 1))
                dve.wait_ge(x_hi_done, n + 1)
                dve.wait_ge(x_staged, n + 1)
                low(a_lo[:, c, cols], bank[n % 2][n // 2 % 2], a_hi[:, c, cols], gains[:, 0, c:c + 1])\
                    .then_inc(x_bank_free, 1)
                if c % 2 == 0:
                    b = n // 2
                    dve.wait_ge(x_half_in[half], 64)
                    if n:
                        dve.drain()
                    nc.vector.tensor_tensor_reduce(out=x_junk[:, :], in0=x_tok[:, b, :], in1=x_tok[:, b, :],
                                                   scale=1.0, scalar=0.0, op0=ALU.mult, op1=ALU.add,
                                                   accum_out=msq[:, b:b + 1])

            def row_factors():
                dve.drain()
                nc.vector.tensor_scalar(chain_v[:, 0:NB], msq[:, :], 1.0 / D, EPS, ALU.mult, ALU.add)
                rsqrt_guess(dve, row_r[:, :], chain_v, NB)
                dve.drain()
                rsqrt_steps(dve, row_r[:, :], chain_v, chain_t, NB)
                return nc.vector.tensor_scalar(msq[:, :], chain_v[:, 0:NB], EPS, None, ALU.mult)

            def wa_split(hq):
                for i in range(4):
                    dve.wait_ge(wa_hi_done, hq * 4 + i + 1)
                    low(wa_lo[:, 2 * i:2 * i + 2, :].rearrange("p k n -> p (k n)"),
                        wa_raw[i][:, :, :, :].rearrange("p k t n -> p (k t n)"),
                        wa_hi[:, 2 * i:2 * i + 2, :].rearrange("p k n -> p (k n)")).then_inc(wa_lo_done, 1)

            wa_split(0)

            dve.wait_ge(const_in, 16 * CONSTS)
            dve.wait_ge(made2, 1)
            nc.vector.tensor_tensor(lam_pr[:, 0:1], lam_in[:, 0:1], lam_in[:, 1:2], ALU.mult)
            nc.vector.tensor_tensor(lam_pr[:, 1:2], lam_in[:, 2:3], lam_in[:, 3:4], ALU.mult)
            nc.vector.tensor_scalar(sink_dg[:, :], ident[0:16, 0:16], sink_col[:, 0:1], None, ALU.mult)
            for i in range(2):
                nc.vector.scalar_tensor_tensor(out=heads64[:, 4 + i:5 + i], in0=heads64[:, 2 * i:2 * i + 1],
                                               scalar=HD ** -0.5, in1=heads64[:, 2 * i + 1:2 * i + 2],
                                               op0=ALU.mult, op1=ALU.mult)
            dve.drain()
            nc.vector.tensor_scalar(k_gain[:, :], k_gain[:, :], heads64[:, 4:5], None, ALU.mult)
            nc.vector.tensor_scalar(gsub[:, :], gsub[:, :], 1.0 - LAM0, None, ALU.mult).then_inc(sinks_done, 1)

            row_factors()
            dve.drain()
            dve.wait_ge(lam_exp, 1)
            nc.vector.tensor_copy(sinks[:, :], proj[:, 16:32])
            nc.vector.tensor_tensor(neg_lam[:, :], lam_e[:, 1:2], lam_e[:, 0:1], ALU.subtract)
            dve.drain()
            nc.vector.tensor_scalar(neg_lam[:, :], neg_lam[:, :], -LAM0, None, ALU.add)
            dve.drain().then_inc(row_stats, 1)

            def head(h, par, attn, tail, qkv, more):
                uses = uses_a(h, attn, tail, qkv)
                hq = h + 1
                for s in range(NB):
                    t = h * NB + s
                    keys = P * (s + 1)
                    if attn:
                        for c, p in ((0, p0[s % 2]), (1, p1)):
                            if c and not qkv:
                                dve.wait_ge(mixed, t)
                            dve.wait_ge(scores_ready, t * 2 + c + 1)
                            dve.sem_inc(dve_passed, 1)
                            nc.vector.tensor_tensor_reduce(
                                out=p[:, 0:keys], in0=score[c][:, 0:keys], in1=dist_a[:, S - keys:S],
                                scale=1.0, scalar=LOWEST, op0=ALU.add, op1=ALU.max,
                                accum_out=mx_a[:, c:c + 1]).then_inc(score_max, 1)
                        dve.wait_ge(score_max, t * 2 + 2)
                        nc.vector.tensor_scalar(nm_a[:, :], mx_a[:, :], one(slopes, h), -1.0, ALU.mult, ALU.mult)\
                            .then_inc(nm_ready, 1)
                    for i in range(2):
                        if ("lag", s, i) in uses:
                            low_wT(uses["lag", s, i], i, (s - 1) % NB, wt_use(h, s, i))
                    if s == 1 and tail:
                        o_factors(h, 1 - par)
                    if attn:
                        dve.wait_ge(exp_done, t * 2 + 2)
                        nc.vector.reciprocal(rcp_a[:, :], ssum[par][:, 1, s:s + 1])
                        dve.drain()
                        nc.vector.scalar_tensor_tensor(out=coef_a[:, :], in0=ssum[par][:, 0, s:s + 1],
                                                       scalar=neg_lam[:, 0:1], in1=rcp_a[:, :],
                                                       op0=ALU.mult, op1=ALU.mult)
                        dve.drain()
                        p = p0[s % 2][:, 0:keys]
                        nc.vector.scalar_tensor_tensor(out=p, in0=p1[:, 0:keys], scalar=coef_a[:, 0:1], in1=p,
                                                       op0=ALU.mult, op1=ALU.add).then_inc(mixed, 1)
                    if qkv:
                        dve.wait_ge(qkv_copied, t + NB + 1)
                        low(v_lo[1 - par][:, s, :], qkv_bank(h, s)[:, 256:384], v_hi[1 - par][:, s, :], row_r[:, s:s + 1])\
                            .then_inc(qkv_free, 1)
                        dve.wait_ge(sq_done, t + NB + 1)
                        m = stat_m[:, 4 * (s % 2):4 * (s % 2) + 4]
                        nc.vector.tensor_reduce(m, sq_a[:, :].rearrange("p (a d) -> p a d", d=HD), AX_X, ALU.add)\
                            .then_inc(red_done, 1)
                        if s % 2 == 0 and (not isinstance(h, int) or h >= 0 or s >= 4):
                            dve.wait_ge(qk_normed, hq * 4 + s // 2 - 1)
                        dve.wait_ge(red_done, t + NB + 1)
                        nc.vector.tensor_scalar(chain_q[s // 2 % 2][:, 4 * (s % 2):4 * (s % 2) + 4], m, 1.0 / HD, msq[:, s:s + 1],
                                                ALU.mult, ALU.add)
                        if s % 2:
                            rsqrt_guess(dve, rstd_qk[s // 2 % 2][:, :], chain_q[s // 2 % 2], 8).then_inc(qk_rstd, 1)

                    if ("pair", s) in uses:
                        b, _, n = uses["pair", s]
                        kp, cols = pair_of(s, par)
                        dve.wait_ge(pair_hi, h * 4 + 4 + s // 2)
                        low(kT_lo[kp][:, cols], trb[b][:, 256:512], kT_hi[kp][:, cols], one(k_gain, h if s == 1 else hq))\
                            .then_inc(kT_done, 1)
                        low(qT_lo[:, cols], trb[b][:, 0:256], qT_hi[:, cols]).then_inc(tr_free[b], 1)
                    if s == NB - 1 and more:
                        wa_split(h + 2)

            def low_wT(use, i, block_s, wt):
                b, _, n = use
                cols = P * (min(4 * i + 4, block_s + 1) - 4 * i)
                view = lambda w: w[:, 4 * i:4 * i + cols // P, :].rearrange("p a n -> p (a n)")
                dve.wait_ge(wT_hi_done, wt + 1)
                low(view(wT_lo), trb[b][:, 0:cols], view(wT_hi)).then_inc(tr_free[b], 1)

            def o_factors(done, par):
                dve.wait_ge(pv_free, done * 2)
                s0 = ssum[par][:, 0, :]
                nc.vector.tensor_tensor(s0sq[:, :], s0, s0, ALU.mult)
                nc.vector.tensor_scalar(chain_o[:, :], oss[:, :], 1.0 / P, None, ALU.mult)
                dve.drain()
                nc.vector.scalar_tensor_tensor(out=chain_o[:, :], in0=s0sq[:, :], scalar=EPS,
                                               in1=chain_o[:, :], op0=ALU.mult, op1=ALU.add)
                rsqrt_guess(dve, rstd_o[:, :], chain_o, NB).then_inc(o_rstd, 1)

            def wt_use(h, s, i):
                block_s = (s - 1) % NB
                before = sum(lag_banks(x) for x in range(block_s))
                return (h - 1 if s == 0 else h) * 12 + before + i

            dve.wait_ge(made3, 1)
            run_heads(dve, head)
            for i in range(2):
                low_wT(last_uses["lag", 0, i], i, NB - 1, wt_use(NH, 0, i))
            o_factors(NH, 1)

            def split_panel(panel, use, slot):
                dve.wait_ge(w_hi_done, panel + 1)
                low(w_lo[slot][:, :, :].rearrange("p k n -> p (k n)"),
                    w_raw[slot][:, :, :].rearrange("p k n -> p (k n)"),
                    w_hi[slot][:, :, :].rearrange("p k n -> p (k n)")).then_inc(w_lo_done, 1)

            def segment(seg):
                def run(kind, panel, use, chunk, quarter, slot, **flags):
                    if not (flags.get("tail") and slot == 1):
                        split_panel(panel + 1, use + slot, 1 - slot)
                    for half in range(2):
                        if kind == "wo":
                            dve.wait_ge(panel_half, panel * 2 + half + 1)
                            x_c = chunk_of(xT, chunk, half)
                            nc.vector.tensor_tensor(x_c, bank[slot][half], x_c, ALU.add)\
                                .then_inc(bank_free[slot][half], 1)
                        elif kind == "up":
                            u = up_half(seg, quarter, chunk, half)
                            dve.wait_ge(u_hi_done, u + 1)
                            dve.wait_ge(u_sq_done, u + 1)
                            low(chunk_of(a_lo, chunk, half), e2[half][:, :], chunk_of(a_hi, chunk, half))\
                                .then_inc(u_split, 1)
                        else:
                            v = up_half(seg, quarter, chunk, half)
                            dve.wait_ge(panel_half, panel * 2 + half + 1)
                            if not isinstance(v, int) or v >= 2:
                                dve.wait_ge(x_added, v - 1)
                            nc.vector.tensor_tensor(e2[half][:, :], bank[slot][half],
                                                    r2[:, HALF * half:HALF * (half + 1)], ALU.mult)\
                                .then_inc(bank_free[slot][half], 1)
                    for half in range(2):
                        if kind == "wo":
                            dve.wait_ge(b_hi_done, chunk * 2 + (32 * seg + half + 1))
                            low(chunk_of(b_lo, chunk, half), chunk_of(xT, chunk, half), chunk_of(b_hi, chunk, half),
                                one(gains[:, 1 + seg, :], chunk)).then_inc(b_split, 1)
                        if kind == "down" and flags.get("last") and seg == 0:
                            dve.wait_ge(b_hi_done, chunk * 2 + (16 + half + 1))
                            low(chunk_of(b_lo, chunk, half), chunk_of(xT, chunk, half), chunk_of(b_hi, chunk, half))\
                                .then_inc(b_split, 1)

                def mlp_factor():
                    for half in range(2):
                        dve.wait_ge(ss_sum, 3 * seg + half + 1)
                        cols = slice(HALF * half, HALF * (half + 1))
                        nc.vector.tensor_scalar(r2[:, cols], (proj, pv)[half][:, :], 1.0 / D, EPS, ALU.mult, ALU.add)
                        dve.drain()
                        nc.vector.reciprocal(r2[:, cols], r2[:, cols])
                    dve.drain().then_inc(r2_ready, 1)

                for c in range(KC):
                    dve.wait_ge(o_split_hi, seg * KC + c + 1)
                    low(a_lo[:, c, :], oT[:, c, :], a_hi[:, c, :]).then_inc(o_split, 1)
                    if c == 0:
                        split_panel(seg * SEG, seg * SEG // 2, 0)
                dve.wait_ge(x_back, 16 * KC * (seg + 1))
                walk(dve, seg, run, before_down=mlp_factor)

            segment(0)

            dve.wait_ge(panel_half, 2 * SEG)
            dve.wait_ge(ss_sum, 3)
            nc.vector.tensor_copy(msq[:, :], proj[:, 0:NB])
            row_factors()
            dve.drain().then_inc(row_stats, 1)

            def wb_split(job, gain):
                for k in range(KC):
                    dve.wait_ge(wb_hi_done, job * KC + k + 1)
                    low(wb_lo[:, k, :], wb_raw[:, k, :], wb_hi[:, k, :], gains[:, gain, k:k + 1])\
                        .then_inc(wb_lo_done, 1)

            def norms(t, s):
                n = t + NB
                vec, out = chain_b[s % 4], rstd_q[s % 4][:, :]
                dve.wait_ge(sqb_done, n + 1)
                nc.vector.tensor_reduce(stat_m[:, 0:4], sq_b[:, :].rearrange("p (a d) -> p a d", d=HD), AX_X,
                                        ALU.add).then_inc(redb_done, 1)
                if not isinstance(t, int) or t >= 4:
                    dve.wait_ge(qb_normed, t - 3)
                dve.wait_ge(redb_done, n + 1)
                nc.vector.tensor_scalar(vec[:, :], stat_m[:, 0:4], 1.0 / HD, msq[:, s % NB:s % NB + 1],
                                        ALU.mult, ALU.add)
                rsqrt_guess(dve, out, vec, 4).then_inc(rstdb, 1)

            wb_split(0, 3)
            for s in range(NB):
                dve.wait_ge(sqb_done, s + 1)
                nc.vector.tensor_reduce(stat_k[:, 4 * s:4 * s + 4], sq_b[:, :].rearrange("p (a d) -> p a d", d=HD),
                                        AX_X, ALU.add).then_inc(redb_done, 1)
            dve.wait_ge(redb_done, NB)
            for s in range(NB):
                nc.vector.tensor_scalar(chain_k[:, 4 * s:4 * s + 4], stat_k[:, 4 * s:4 * s + 4], 1.0 / HD,
                                        msq[:, s:s + 1], ALU.mult, ALU.add)
            rsqrt_guess(dve, rstd_k[:, :, :].rearrange("p a b -> p (a b)"), chain_k, NB * KVH).then_inc(rstdb, 1)
            wb_split(1, 3)
            for s in range(NB):
                dve.wait_ge(vb_hi_done, s + 1)
                low(vb[:, s, :, 1, :], proj_bank(NB + s)[:, 0:256].rearrange("p (a d) -> p a d", d=HD),
                    vb[:, s, :, 0, :], row_r[:, s:s + 1]).then_inc(pb_free, 1)

            def steps(g, lag, proj_on, which, more=True):
                uses = uses_b(g, lag, proj_on, which)
                for s in which:
                    t = g * NB + s
                    prev = (s >= 1 or lag) and (proj_on or s == 0)
                    if prev:
                        par = (s - 1) % 2
                        dve.wait_ge(qt_hi, t)
                        low(qTb_lo[par][:, :, :].rearrange("p a n -> p (a n)"), score[1][:, 0:256],
                            qTb_hi[par][:, :, :].rearrange("p a n -> p (a n)")).then_inc(qt_free, 1)
                    for b in range(2):
                        if ("p", s, b) in uses:
                            dve.wait_ge(bm_hi[b], uses["p", s, b] + 1)
                            low(wTb_lo[:, b, :], trb[b][:, :], wTb_hi[:, b, :]).then_inc(bm_free[b], 1)
                    if prev:
                        lo = P if s == 1 else CH
                        g_p = g if s else g - 1
                        dve.wait_ge(sb_ready, t)
                        if s == 1:
                            dve.wait_ge(biasb_ready, g * GRP + GRP)
                        dve.sem_inc(dve_passed, 1)
                        for j in range(GRP):
                            nc.vector.tensor_tensor_reduce(
                                out=pb[par][:, j, lo:256], in0=score_cols(j, lo),
                                in1=bias_b[:, j, lo:256], scale=1.0, scalar=LOWEST, op0=ALU.add, op1=ALU.max,
                                accum_out=mx_b[:, j:j + 1])
                        dve.drain().then_inc(sb_max, 1)
                        sk = sinks[:, bass.ds(g_p * GRP, GRP)]
                        nc.vector.tensor_tensor(mx_b[:, :], mx_b[:, :], sk, ALU.max)
                        dve.drain()
                        nc.vector.tensor_tensor(esin_b[par][:, :], sk, mx_b[:, :], ALU.subtract)
                        nc.vector.tensor_scalar(nm_b[par][:, :], mx_b[:, :], -1.0, None, ALU.mult)\
                            .then_inc(nmb_ready, 1)
                    if proj_on and (s < NB - 1 or more):
                        norms(t + 1, s + 1)
                        if s == NB - 2 and more:
                            wb_split(g + 3, 4)
                    if (s >= 2 or lag) and (proj_on or s < 2):
                        par = s % 2
                        dve.wait_ge(expb_done, t - 1)
                        nc.vector.tensor_tensor(den_b[:, :], sm_b[par][:, :], es_b[par][:, :], ALU.add)
                        dve.drain()
                        nc.vector.reciprocal(rc_b[:, :], den_b[:, :])
                        dve.drain()
                        dve.wait_ge(pvb_ready, t - 1)
                        o = pv[:, :].rearrange("p (a b d) -> p a d b", b=2, d=HD)
                        nc.vector.tensor_reduce(osum[:, :, :], o, AX_X, ALU.add)\
                            .then_inc(pvb_free, 1)
                        dve.drain()
                        nc.vector.tensor_tensor(osb[par][:, :, :], osum[:, :, :],
                                                rc_b[:, :].unsqueeze(2).to_broadcast([P, GRP, HD]), ALU.mult)\
                            .then_inc(osb_ready, 1)
                    if ("k", 0) in uses and s == 0:
                        for b in range(2):
                            dve.wait_ge(bm_hi[b], uses["k", b] + 1)
                            low(kTb_lo[:, HALF * b:HALF * (b + 1)], trb[b][:, :], kTb_hi[:, HALF * b:HALF * (b + 1)],
                                heads64[:, 5:6]).then_inc(bm_free[b], 1)

            dve.wait_ge(pz, 2)
            wb_split(2, 4)
            norms(0, 0)
            steps(0, False, True, range(NB))
            with dve.Fori(1, KVH - 1) as g:
                steps(g, True, True, range(NB))
            steps(KVH - 1, True, True, range(NB), more=False)
            steps(KVH, True, False, range(3))
            segment(1)


        @block.tensor
        def _(pe):
            def mm(out, a, b, start, stop, **kw):
                return nc.tensor.matmul(out, a, b, start=start, stop=stop, **kw)

            def three(out, a, b, start, stop):
                mm(out, a[0], b[0], start, False)
                mm(out, a[0], b[1], False, False)
                return mm(out, a[1], b[0], False, stop)

            pe.wait_ge(made2, 1)
            for n in range(2 * KC):
                half, c = divmod(n, KC)
                if c == 0:
                    pe.wait_ge(x_half_in[half], 64)
                if n >= 4:
                    pe.wait_ge(x_bank_free, n - 3)
                for b in range(4):
                    last = nc.tensor.transpose(bank[n % 2][n // 2 % 2][:, P * b:P * (b + 1)],
                                               x_tok[:, 4 * half + b, P * c:P * (c + 1)], ident[:, :])
                last.then_inc(x_tr, 1)

            def small_products():
                pe.wait_ge(sinks_done, 1)
                mm(proj[:, 0:2], ones[0:HD, :], lam_pr[:, :], True, True)
                mm(proj[:, 16:32], ones[0:16, :], sink_dg[:, :], True, True).then_inc(small_mm, 1)

            def bank_for(b, before):
                if not isinstance(before, int) or before > 0:
                    pe.wait_ge(tr_free[b], before)

            def transpose_weights(uses, s, block_s, tw):
                pe.wait_ge(mixed, tw + 1)
                for i in range(lag_banks(block_s)):
                    b, before, n = uses["lag", s, i]
                    bank_for(b, before)
                    for kc in range(4 * i, min(4 * i + 4, block_s + 1)):
                        last = nc.tensor.transpose(trb[b][:, P * (kc - 4 * i):P * (kc - 4 * i + 1)],
                                                   p0[block_s % 2][:, P * kc:P * (kc + 1)], ident[:, :])
                    last.then_inc(tr_ready, 1)

            def values(uses, s, block_s, done, vp):
                for i in range(lag_banks(block_s)):
                    b, before, _ = uses["lag", s, i]
                    pe.wait_ge(tr_free[b], before + 1)
                if block_s % 4 == 0 and (not isinstance(done, int) or done > 0):
                    pe.wait_ge(pv_free, done)
                at = P * (block_s % 4)
                for kc in range(block_s + 1):
                    last = three(pv[:, at:at + P], (wT_hi[:, kc, :], wT_lo[:, kc, :]),
                                 (v_hi[vp][:, kc, :], v_lo[vp][:, kc, :]), kc == 0, kc == block_s)
                last.then_inc(pv_ready, 1)

            def transpose_outputs(uses, done):
                pe.wait_ge(o_normed, done)
                for i in range(2):
                    b, before, _ = uses["o", i]
                    bank_for(b, before)
                    for s in range(4):
                        last = nc.tensor.transpose(trb[b][:, P * s:P * (s + 1)], oraw[:, 4 * i + s, :], ident[:, :])
                    last.then_inc(tr_ready, 1)

            def head(h, par, attn, tail, qkv, more):
                uses = uses_a(h, attn, tail, qkv)
                for s in range(NB):
                    t = h * NB + s
                    if attn:
                        if s % 2 == 0:
                            pe.wait_ge(kT_done, h * 4 + s // 2 + 1)
                        for c in range(2):
                            rows = slice(HD * c, HD * (c + 1))
                            if not isinstance(h, int) or h or s:
                                pe.wait_ge(score_max, t * 2 + c - 1)
                            for k0 in range(0, P * (s + 1), HALF):
                                k1 = min(k0 + HALF, P * (s + 1))
                                q = slice(P * s, P * (s + 1))
                                last = three(score[c][:, k0:k1], (qT_hi[rows, q], qT_lo[rows, q]),
                                             (kT_hi[par][rows, k0:k1], kT_lo[par][rows, k0:k1]), True, True)
                            last.then_inc(scores_ready, 1)
                    lag = ("lag", s, 0) in uses
                    if lag:
                        transpose_weights(uses, s, (s - 1) % NB, t - 1)
                    if qkv:
                        if not isinstance(h, int) or h >= 0:
                            pe.wait_ge(qkv_free, t + NB)
                        elif s >= 2:
                            pe.wait_ge(qkv_free, s - 1)
                        elif s == 1:
                            pe.wait_ge(row_stats, 1)
                        for k in range(KC):
                            if s == 0 and k % 2 == 0:
                                pe.wait_ge(wa_lo_done, h * 4 + 4 + k // 2 + 1)
                            tok = slice(P * s, P * (s + 1))
                            last = three(qkv_bank(h, s)[:, 0:384], (a_hi[:, k, tok], a_lo[:, k, tok]),
                                         (wa_hi[:, k, :], wa_lo[:, k, :]), k == 0, k == KC - 1)
                        last.then_inc(qkv_ready, 1)
                        if isinstance(h, int) and h < 0 and s == 0:
                            small_products()
                    if ("pair", s) in uses:
                        b, before, _ = uses["pair", s]
                        pe.wait_ge(qk_normed, h * 4 + 4 + s // 2)
                        bank_for(b, before)
                        for i in range(4):
                            last = nc.tensor.transpose(trb[b][:, P * i:P * (i + 1)],
                                                       qk2[:, (s - 3) % 4 + i % 2, P * (i // 2):P * (i // 2 + 1)],
                                                       ident[:, :])
                        last.then_inc(tr_ready, 1)
                    if s == O_STEP and tail:
                        transpose_outputs(uses, h)
                    if lag:
                        values(uses, s, (s - 1) % NB, h * 2 + (s - 1) // 4, par if s else 1 - par)

            run_heads(pe, head)
            transpose_weights(last_uses, 0, NB - 1, NH * NB - 1)
            values(last_uses, 0, NB - 1, NH * 2 - 1, 1)
            transpose_outputs(last_uses, NH)

            def segment(seg):
                def run(kind, panel, use, chunk, quarter, slot, **flags):
                    x_hi, x_lo = (b_hi, b_lo) if kind == "up" else (a_hi, a_lo)
                    pe.wait_ge(w_lo_done, panel + 1)
                    for half in range(2):
                        if not isinstance(panel, int) or panel >= 2:
                            pe.wait_ge(bank_free[slot][half], use)
                    for k in range(KC):
                        if kind == "wo":
                            pe.wait_ge(o_split, seg * KC + k + 1)
                        if kind == "up" and flags.get("first"):
                            pe.wait_ge(b_split, 32 * seg + 2 * k + 2)
                        if kind == "down" and k in (0, 6, 7):
                            pe.wait_ge(u_split, seg * 64 + quarter * 16 + (12 if k == 0 else 2 * k + 2))
                        w_h, w_l = w_hi[slot][:, k, :], w_lo[slot][:, k, :]
                        first, last = k == 0, k == KC - 1
                        out = bank[slot]
                        xs = [(x_hi[:, k, HALF * i:HALF * (i + 1)], x_lo[:, k, HALF * i:HALF * (i + 1)])
                              for i in range(2)]
                        if last:
                            for i in range(2):
                                three(out[i], (w_h, w_l), xs[i], False, True).then_inc(panel_half, 1)
                            continue
                        for i in range(2):
                            mm(out[i], w_h, xs[i][0], first, False)
                            mm(out[i], w_h, xs[i][1], False, False)
                        for i in range(2):
                            mm(out[i], w_l, xs[i][0], False, False)
                    if kind == "down" and flags.get("last") and seg == 1:
                        if slot or not flags.get("head"):
                            transpose_out(chunk - 1)
                        if flags.get("tail") and slot:
                            transpose_out(chunk)

                def transpose_out(chunk):
                    for half in range(2):
                        n = out_index(chunk, half)
                        pe.wait_ge(x_added, 64 + 48 + n + 1)
                        if not isinstance(n, int) or n >= 2:
                            pe.wait_ge(out_staged, n - 1)
                        for b in range(4):
                            last = nc.tensor.transpose((proj, pv)[half][:, P * b:P * (b + 1)],
                                                       e1[half][:, P * b:P * (b + 1)], ident[:, :])
                        last.then_inc(out_tr, 1)

                def sum_squares():
                    pe.wait_ge(ss_added, 18 + 36 * seg)
                    for half in range(2):
                        mm((proj, pv)[half][:, :], ones[:, :], ss[:, HALF * half:HALF * (half + 1)], True, True)\
                            .then_inc(ss_sum, 1)

                walk(pe, seg, run, before_down=sum_squares)

            segment(0)

            pe.wait_ge(ss_added, 36)
            pe.wait_ge(r2_ready, 1)
            for b in range(NB):
                last = mm(proj[:, b:b + 1], ss[:, P * b:P * (b + 1)], ones[:, 0:1], True, True)
            last.then_inc(ss_sum, 1)
            pe.wait_ge(row_stats, 2)

            def project(job, s, between=None):
                n = job * NB + s
                if not isinstance(job, int) or n >= 2 * NB:
                    pe.wait_ge(pb_free, n)
                elif n >= 2:
                    pe.wait_ge(pb_free, n - 1)
                for k in range(KC):
                    if s == 0:
                        pe.wait_ge(wb_lo_done, job * KC + k + 1)
                        if isinstance(job, int) and job == 0:
                            pe.wait_ge(b_split, 16 + 2 * k + 2)
                    tok = slice(P * s, P * (s + 1))
                    if k == 5 and between:
                        between()
                    last = three(proj_bank(n)[:, 0:256], (b_hi[:, k, tok], b_lo[:, k, tok]),
                                 (wb_hi[:, k, :], wb_lo[:, k, :]), k == 0, k == KC - 1)
                last.then_inc(pb_ready, 1)

            for job in range(2):
                for s in range(NB):
                    project(job, s)

            def steps(g, lag, proj_on, which, more=True):
                uses = uses_b(g, lag, proj_on, which)
                for s in which:
                    t = g * NB + s
                    prev = (s >= 1 or lag) and (proj_on or s == 0)

                    def transpose_q():
                        pe.wait_ge(qb_normed, t)
                        if not isinstance(g, int) or t >= 2:
                            pe.wait_ge(qt_free, t - 1)
                        for a in range(2):
                            last = nc.tensor.transpose(score[1][:, P * a:P * (a + 1)],
                                                       qraw_b[(s - 1) % 4][:, P * a:P * (a + 1)], ident[:, :])
                        last.then_inc(qt_ready, 1)

                    def transpose_both():
                        if prev:
                            transpose_q()
                        if (s >= 2 or lag) and (proj_on or s < 2):
                            pe.wait_ge(expb_done, t - 1)
                            for b in range(2):
                                if ("p", s, b) not in uses:
                                    continue
                                before = uses["p", s, b]
                                if not isinstance(before, int) or before > 0:
                                    pe.wait_ge(bm_free[b], before)
                                for j in range(GRP):
                                    last = nc.tensor.transpose(trb[b][:, P * j:P * (j + 1)],
                                                               pb[s % 2][:, j, P * b:P * (b + 1)], ident[:, :])
                                last.then_inc(bm_ready[b], 1)

                    if proj_on and (s < NB - 1 or more):
                        project(g + 2 + (s + 1) // NB, (s + 1) % NB, transpose_both)
                    else:
                        transpose_both()
                    if prev:
                        par, blk = (s - 1) % 2, (s - 1) % NB
                        pe.wait_ge(qt_free, t)
                        if not isinstance(g, int) or t >= 2:
                            pe.wait_ge(sb_max, t - 1)
                        if s == 1:
                            for b in range(2):
                                pe.wait_ge(bm_free[b], uses["k", b] + 1)
                        lo = P if blk == 0 else CH
                        keys = slice(P * (blk - 1) + lo, P * (blk + 1))
                        for j in range(GRP):
                            rows = slice(HD * (j % 2), HD * (j % 2 + 1))
                            last = three(score_cols(j, lo),
                                         (qTb_hi[par][rows, j // 2, :], qTb_lo[par][rows, j // 2, :]),
                                         (kTb_hi[rows, keys], kTb_lo[rows, keys]), True, True)
                        last.then_inc(sb_ready, 1)
                    if (s >= 2 or lag) and (proj_on or s < 2):
                        blk = (s - 2) % NB
                        g_v = g if s >= 2 else g - 1
                        if not isinstance(g, int) or t > 2:
                            pe.wait_ge(pvb_free, t - 2)
                        for b in range(2):
                            if ("p", s, b) in uses:
                                pe.wait_ge(bm_free[b], uses["p", s, b] + 1)
                        kcs = [1] if blk == 0 else [0, 1]
                        for j in range(GRP):
                            for kc in kcs:
                                v = vb[:, blk - 1 + kc, bass.ds(g_v, 1), :, :].rearrange("p a b d -> p (a b d)")
                                for part in (wTb_hi, wTb_lo):
                                    last = mm(pv[:, P * j:P * (j + 1)], part[:, kc, P * j:P * (j + 1)], v,
                                              kc == kcs[0] and part is wTb_hi, kc == 1 and part is wTb_lo)
                        last.then_inc(pvb_ready, 1)
                    if s >= 3 or lag:
                        pe.wait_ge(osb_ready, t - 2)
                        if not isinstance(g, int) or t > 3:
                            pe.wait_ge(ot_free, t - 3)
                        for a in range(2):
                            last = nc.tensor.transpose(
                                score[1][:, HALF + P * a:HALF + P * (a + 1)],
                                osb[(s - 3) % 2][:, 2 * a:2 * a + 2, :].rearrange("p a d -> p (a d)"), ident[:, :])
                        last.then_inc(ot_ready, 1)
                    if ("k", 0) in uses and s == 0:
                        pe.wait_ge(kn_ready, g * 2 + 2)
                        for b in range(2):
                            before = uses["k", b]
                            if not isinstance(before, int) or before > 0:
                                pe.wait_ge(bm_free[b], before)
                            for i in range(4):
                                last = nc.tensor.transpose(
                                    trb[b][:, P * i:P * (i + 1)],
                                    kn[:, 4 * b + i, :, :].rearrange("p a d -> p (a d)"), ident[:, :])
                            last.then_inc(bm_ready[b], 1)

            project(2, 0)
            steps(0, False, True, range(NB))
            with pe.Fori(1, KVH - 1) as g:
                steps(g, True, True, range(NB))
            steps(KVH - 1, True, True, range(NB), more=False)
            steps(KVH, True, False, range(3))
            segment(1)


_INS = ["x", "attn_norm_g", "mlp_norm_g", "a_w_qkv", "a_q_norm_g", "a_k_norm_g", "a_lambda_q1", "a_lambda_k1",
        "a_lambda_q2", "a_lambda_k2", "a_subln_g", "a_w_o", "kv_norm_g", "w_kv", "kv_k_norm_g", "b_w_q",
        "b_q_norm_g", "b_sinks", "b_w_o", "mlp_w_up", "mlp_w_down"]


def kernel(**inputs):
    import numpy as _np
    import concourse.bacc as _bacc
    from concourse import mybir as _mybir
    from concourse.bass_utils import run_bass_kernel_spmd as _run

    nc = _bacc.Bacc("TRN2", target_bir_lowering=False, num_devices=1)
    arrays, io = {}, {}
    for name in _INS:
        a = _np.ascontiguousarray(inputs[name])
        arrays[f"in_{name}"] = a
        io[name] = nc.dram_tensor(f"in_{name}", a.shape, _mybir.dt.from_np(a.dtype), kind="ExternalInput").ap()
    io["out"] = nc.dram_tensor("out", (1, S, D), F32, kind="ExternalOutput").ap()
    trunk(nc, io)
    r = _run(nc, [arrays], core_ids=[0])
    return r.results[0]["out"]
```
